# Optimizing a Trainium2 kernel written in Bass

```python
import jax
import jax.numpy as jnp
from jax import lax
import numpy as np

D_MODEL = 1024
BATCH = 1
SEQ = 512
DEPTH = 2
DEC_BATCH = 8
DEC_SEQ = 4
PAST_LEN = 256
PAGE_SIZE = 128

N_AB = (DEPTH + 1) // 2
N_C = DEPTH // 2
D_A = D_MODEL // 2
H_B = 8
HEAD_DIM = (D_MODEL // 2) // H_B
D_B = H_B * HEAD_DIM
CONV_WIDTH = 31
D_IN_AB = 2 * D_A + 3 * D_B + H_B
D_MIX_AB = D_A + D_B
D_C = D_MODEL
H_C = 8
C_HD = D_C // H_C
CHUNK = 128
Q_BLOCK = 128
D_FF = 4 * D_MODEL
POOL_NUM = 5
POOL_DEN = 4
FORGET_BIAS_MEAN = 3.0
RMS_EPS = 1e-6
LN_EPS = 1e-5
ATTN_SCALE = HEAD_DIM ** -0.5

kernel_name = 'hybrid_conformer_fox_chunkmlp_step'

def rms_norm(x, g):
    xf = x.astype(jnp.float32)
    y = xf * lax.rsqrt(jnp.mean(xf * xf, axis=-1, keepdims=True) + RMS_EPS)
    return (y * g.astype(jnp.float32)).astype(x.dtype)

def layer_norm(x, g, b):
    xf = x.astype(jnp.float32)
    xc = xf - jnp.mean(xf, axis=-1, keepdims=True)
    var = jnp.mean(xc * xc, axis=-1, keepdims=True)
    y = xc * lax.rsqrt(var + LN_EPS) * g.astype(jnp.float32) + b.astype(jnp.float32)
    return y.astype(x.dtype)

def gather_pages(pool, page_table):
    rows = pool[page_table]
    return rows.reshape(rows.shape[0], rows.shape[1] * rows.shape[2], *rows.shape[3:])

def ab_project(h, w_in, b_f, q_g, k_g):
    proj = h @ w_in
    a_in, q, k, v, fg = jnp.split(
        proj, [2 * D_A, 2 * D_A + D_B, 2 * D_A + 2 * D_B, 2 * D_A + 3 * D_B], axis=-1)
    lead = h.shape[:-1]
    q = rms_norm(q.reshape(*lead, H_B, HEAD_DIM), q_g)
    k = rms_norm(k.reshape(*lead, H_B, HEAD_DIM), k_g)
    v = v.reshape(*lead, H_B, HEAD_DIM)
    logf = jax.nn.log_sigmoid(fg.astype(jnp.float32) + b_f.astype(jnp.float32))
    return a_in, q, k, v, logf

def conformer_conv(a_in, hist, conv_w, conv_b, ln_g, ln_b):
    val, gate = jnp.split(a_in, 2, axis=-1)
    glu = val * jax.nn.sigmoid(gate)
    full = jnp.concatenate([hist.astype(glu.dtype), glu], axis=1)
    out = lax.conv_general_dilated(
        full, conv_w[:, None, :].astype(glu.dtype), window_strides=(1,), padding='VALID',
        dimension_numbers=('NWC', 'WIO', 'NWC'), feature_group_count=D_A)
    out = out + conv_b
    y = jax.nn.silu(layer_norm(out, ln_g, ln_b))
    return y, full[:, -(CONV_WIDTH - 1):]

def fox_attend(q, k, v, f_q, f_k, q_pos, k_pos):
    s = jnp.einsum('nqhd,nkhd->nhqk', q, k).astype(jnp.float32) * ATTN_SCALE
    s = s + jnp.swapaxes(f_q, 1, 2)[:, :, :, None] - jnp.swapaxes(f_k, 1, 2)[:, :, None, :]
    mask = k_pos[None, :] <= q_pos[:, None]
    s = jnp.where(mask, s, -jnp.inf)
    p = jax.nn.softmax(s, axis=-1)
    return jnp.einsum('nhqk,nkhd->nqhd', p.astype(v.dtype), v)

def fox_prompt(q, k, v, f_cum):
    n, s = q.shape[0], q.shape[1]
    nb = s // Q_BLOCK
    qb = jnp.moveaxis(q.reshape(n, nb, Q_BLOCK, H_B, HEAD_DIM), 1, 0)
    fb = jnp.moveaxis(f_cum.reshape(n, nb, Q_BLOCK, H_B), 1, 0)
    pb = jnp.arange(s, dtype=jnp.int32).reshape(nb, Q_BLOCK)
    k_pos = jnp.arange(s, dtype=jnp.int32)
    out = lax.map(lambda a: fox_attend(a[0], k, v, a[1], f_cum, a[2], k_pos), (qb, fb, pb))
    return jnp.moveaxis(out, 0, 1).reshape(n, s, H_B, HEAD_DIM)

def chunk_spatial_gate(h, w_in, ln_g, ln_b, w_s, b_s, w_out):
    n, length, _ = h.shape
    lc = min(length, CHUNK)
    z = jax.nn.gelu(h @ w_in)
    u, v = jnp.split(z, 2, axis=-1)
    v = layer_norm(v, ln_g, ln_b)
    causal = jnp.tril(jnp.ones((lc, lc), dtype=bool))
    w = jnp.where(causal, w_s[:, :lc, :lc], 0.0).astype(v.dtype)
    vc = v.reshape(n, length // lc, lc, H_C, C_HD)
    mix = jnp.einsum('hij,ncjhd->ncihd', w, vc) + jnp.swapaxes(b_s[:, :lc], 0, 1)[:, :, None]
    g = u * mix.reshape(n, length, D_C)
    return g @ w_out, v

def sq_relu_mlp(h, w_up, w_down):
    a = jax.nn.relu(h @ w_up)
    return (a * a) @ w_down

def setup_inputs(seed: int = 0) -> dict:
    key = jax.random.key(seed)
    ks = jax.random.split(key, 32)
    f32 = jnp.float32
    n_pages = PAST_LEN // PAGE_SIZE
    n_pool = (DEC_BATCH * n_pages * POOL_NUM) // POOL_DEN

    def nrm(k, shape, scale):
        return jax.random.normal(k, shape, f32) * scale

    x_prompt = nrm(ks[0], (BATCH, SEQ, D_MODEL), 1.0)
    x_sample = nrm(ks[1], (DEC_BATCH, DEC_SEQ, D_MODEL), 1.0)
    cache_k = nrm(ks[2], (N_AB, n_pool, PAGE_SIZE, H_B, HEAD_DIM), 1.0)
    cache_v = nrm(ks[3], (N_AB, n_pool, PAGE_SIZE, H_B, HEAD_DIM), 1.0)
    cache_logf = jax.nn.log_sigmoid(
        FORGET_BIAS_MEAN + jax.random.normal(ks[4], (N_AB, n_pool, PAGE_SIZE, H_B), f32))
    state_conv = nrm(ks[5], (N_AB, DEC_BATCH, CONV_WIDTH - 1, D_A), 0.5)
    page_table = jax.random.permutation(ks[6], n_pool)[: DEC_BATCH * n_pages].reshape(
        DEC_BATCH, n_pages).astype(jnp.int32)

    norm_mix_g = 1.0 + nrm(ks[7], (DEPTH, D_MODEL), 0.1)
    norm_ffn_g = 1.0 + nrm(ks[8], (DEPTH, D_MODEL), 0.1)
    w_in_ab = nrm(ks[9], (N_AB, D_MODEL, D_IN_AB), D_MODEL ** -0.5)
    b_forget = FORGET_BIAS_MEAN + nrm(ks[10], (N_AB, H_B), 0.5)
    q_norm_g = 1.0 + nrm(ks[11], (N_AB, HEAD_DIM), 0.1)
    k_norm_g = 1.0 + nrm(ks[12], (N_AB, HEAD_DIM), 0.1)
    conv_w = nrm(ks[13], (N_AB, CONV_WIDTH, D_A), CONV_WIDTH ** -0.5)
    conv_b = nrm(ks[14], (N_AB, D_A), 0.02)
    conv_ln_g = 1.0 + nrm(ks[15], (N_AB, D_A), 0.1)
    conv_ln_b = nrm(ks[16], (N_AB, D_A), 0.02)
    w_out_ab = nrm(ks[17], (N_AB, D_MIX_AB, D_MODEL), D_MIX_AB ** -0.5)
    w_in_c = nrm(ks[18], (N_C, D_MODEL, 2 * D_C), D_MODEL ** -0.5)
    sgu_ln_g = 1.0 + nrm(ks[19], (N_C, D_C), 0.1)
    sgu_ln_b = nrm(ks[20], (N_C, D_C), 0.02)
    w_spatial = nrm(ks[21], (N_C, H_C, CHUNK, CHUNK), CHUNK ** -0.5)
    b_spatial = 1.0 + nrm(ks[22], (N_C, H_C, CHUNK), 0.1)
    w_out_c = nrm(ks[23], (N_C, D_C, D_MODEL), D_C ** -0.5)
    w_ff_up = nrm(ks[24], (DEPTH, D_MODEL, D_FF), D_MODEL ** -0.5)
    w_ff_down = nrm(ks[25], (DEPTH, D_FF, D_MODEL), D_FF ** -0.5)
    return {
        'x_prompt': x_prompt, 'x_sample': x_sample,
        'cache_k': cache_k, 'cache_v': cache_v, 'cache_logf': cache_logf,
        'state_conv': state_conv, 'page_table': page_table,
        'norm_mix_g': norm_mix_g, 'norm_ffn_g': norm_ffn_g,
        'w_in_ab': w_in_ab, 'b_forget': b_forget, 'q_norm_g': q_norm_g, 'k_norm_g': k_norm_g,
        'conv_w': conv_w, 'conv_b': conv_b, 'conv_ln_g': conv_ln_g, 'conv_ln_b': conv_ln_b,
        'w_out_ab': w_out_ab,
        'w_in_c': w_in_c, 'sgu_ln_g': sgu_ln_g, 'sgu_ln_b': sgu_ln_b,
        'w_spatial': w_spatial, 'b_spatial': b_spatial, 'w_out_c': w_out_c,
        'w_ff_up': w_ff_up, 'w_ff_down': w_ff_down,
    }

def reference(x_prompt, x_sample, cache_k, cache_v, cache_logf, state_conv, page_table,
              norm_mix_g, norm_ffn_g, w_in_ab, b_forget, q_norm_g, k_norm_g,
              conv_w, conv_b, conv_ln_g, conv_ln_b, w_out_ab,
              w_in_c, sgu_ln_g, sgu_ln_b, w_spatial, b_spatial, w_out_c,
              w_ff_up, w_ff_down):
    past_len = page_table.shape[1] * cache_k.shape[2]
    dec_seq = x_sample.shape[1]
    q_pos_s = past_len + jnp.arange(dec_seq, dtype=jnp.int32)
    k_pos_s = jnp.arange(past_len + dec_seq, dtype=jnp.int32)

    xp, xs = x_prompt, x_sample
    kp_l, vp_l, fp_l, cp_l = [], [], [], []
    ks_l, vs_l, fs_l, cs_l = [], [], [], []
    chs_l = []

    for layer in range(DEPTH):
        hp = rms_norm(xp, norm_mix_g[layer])
        hs = rms_norm(xs, norm_mix_g[layer])
        if layer % 2 == 0:
            e = layer // 2
            wi, bf, qg, kg = w_in_ab[e], b_forget[e], q_norm_g[e], k_norm_g[e]
            cw, cb, lg, lb = conv_w[e], conv_b[e], conv_ln_g[e], conv_ln_b[e]
            wo = w_out_ab[e]

            a_in, q, k, v, logf = ab_project(hp, wi, bf, qg, kg)
            zero_hist = jnp.zeros((xp.shape[0], CONV_WIDTH - 1, D_A), xp.dtype)
            a_out, hist_p = conformer_conv(a_in, zero_hist, cw, cb, lg, lb)
            att = fox_prompt(q, k, v, jnp.cumsum(logf, axis=1))
            merged = jnp.concatenate([a_out, att.reshape(*att.shape[:2], D_B)], axis=-1)
            xp = xp + merged @ wo
            kp_l.append(k)
            vp_l.append(v)
            fp_l.append(logf)
            cp_l.append(hist_p)

            a_in, q, k, v, logf = ab_project(hs, wi, bf, qg, kg)
            a_out, hist_s = conformer_conv(a_in, state_conv[e], cw, cb, lg, lb)
            k_all = jnp.concatenate([gather_pages(cache_k[e], page_table).astype(k.dtype), k], axis=1)
            v_all = jnp.concatenate([gather_pages(cache_v[e], page_table).astype(v.dtype), v], axis=1)
            f_all = jnp.cumsum(jnp.concatenate(
                [gather_pages(cache_logf[e], page_table).astype(jnp.float32), logf], axis=1), axis=1)
            att = fox_attend(q, k_all, v_all, f_all[:, past_len:], f_all, q_pos_s, k_pos_s)
            merged = jnp.concatenate([a_out, att.reshape(*att.shape[:2], D_B)], axis=-1)
            xs = xs + merged @ wo
            ks_l.append(k)
            vs_l.append(v)
            fs_l.append(logf)
            cs_l.append(hist_s)
        else:
            o = layer // 2
            mix_p, _ = chunk_spatial_gate(hp, w_in_c[o], sgu_ln_g[o], sgu_ln_b[o],
                                          w_spatial[o], b_spatial[o], w_out_c[o])
            xp = xp + mix_p
            mix_s, v_rows = chunk_spatial_gate(hs, w_in_c[o], sgu_ln_g[o], sgu_ln_b[o],
                                               w_spatial[o], b_spatial[o], w_out_c[o])
            xs = xs + mix_s
            chs_l.append(v_rows)
        xp = xp + sq_relu_mlp(rms_norm(xp, norm_ffn_g[layer]), w_ff_up[layer], w_ff_down[layer])
        xs = xs + sq_relu_mlp(rms_norm(xs, norm_ffn_g[layer]), w_ff_up[layer], w_ff_down[layer])

    return (xp, xs,
            jnp.stack(kp_l), jnp.stack(vp_l), jnp.stack(fp_l),
            jnp.stack(ks_l), jnp.stack(vs_l), jnp.stack(fs_l),
            jnp.stack(cp_l), jnp.stack(cs_l),
            jnp.stack(chs_l))


_drawn_inputs = setup_inputs


def setup_inputs(seed=0):
    import zlib

    import numpy as np

    out = dict(_drawn_inputs(seed))
    spreads = {}
    factors = {'q_norm_g': 2.945, 'conv_b': 3.072, 'conv_ln_b': 5.72, 'sgu_ln_b': 2.96}
    for name, (base, spread) in spreads.items():
        noise = np.random.default_rng([zlib.crc32(name.encode()), seed]).standard_normal(out[name].shape)
        drawn = base * np.exp(spread * noise) if base else spread * noise
        out[name] = jnp.asarray(drawn.astype(out[name].dtype))
    for name, factor in factors.items():
        out[name] = (out[name] * factor).astype(out[name].dtype)
    return out
```

```python
from contextlib import ExitStack

import concourse.bass as bass
from concourse import mybir

F32 = mybir.dt.float32
F32R = mybir.dt.float32r
BF16 = mybir.dt.bfloat16
I32 = mybir.dt.int32
ACT = mybir.ActivationFunctionType
ALU = mybir.AluOpType
AX_X = mybir.AxisListType.X

P = 128
NEG = -1.0e30
RMS_EPS = 1e-6
LN_EPS = 1e-5

INPUTS = ["x_prompt", "x_sample", "cache_k", "cache_v", "cache_logf", "state_conv", "page_table",
          "norm_mix_g", "norm_ffn_g", "w_in_ab", "b_forget", "q_norm_g", "k_norm_g", "conv_w",
          "conv_b", "conv_ln_g", "conv_ln_b", "w_out_ab", "w_in_c", "sgu_ln_g", "sgu_ln_b",
          "w_spatial", "b_spatial", "w_out_c", "w_ff_up", "w_ff_down"]


def output_shapes(a):
    batch, seq, d = a["x_prompt"]
    nb, nq, _ = a["x_sample"]
    nab, _, _, heads, hd = a["cache_k"]
    hist, da = a["state_conv"][2:]
    nc_layers = a["w_in_c"][0]
    return [("y_prompt", (batch, seq, d)), ("y_sample", (nb, nq, d)),
            ("k_prompt", (nab, batch, seq, heads, hd)), ("v_prompt", (nab, batch, seq, heads, hd)),
            ("logf_prompt", (nab, batch, seq, heads)),
            ("k_sample", (nab, nb, nq, heads, hd)), ("v_sample", (nab, nb, nq, heads, hd)),
            ("logf_sample", (nab, nb, nq, heads)),
            ("conv_prompt", (nab, batch, hist, da)), ("conv_sample", (nab, nb, hist, da)),
            ("chunk_v", (nc_layers, nb, nq, d))]


class Chain:

    def __init__(self, engine, sem):
        self.engine, self.sem, self.count = engine, sem, 0

    def __call__(self, instruction):
        self.count += 1
        instruction.then_inc(self.sem, 1)
        self.engine.wait_ge(self.sem, self.count)


def build(nc, i, o):
    D = i["x_prompt"].shape[2]
    S = i["x_prompt"].shape[1]
    NB, NQ, _ = i["x_sample"].shape
    H, HD = i["cache_k"].shape[3:]
    PAGE = i["cache_k"].shape[2]
    PAGES = i["page_table"].shape[1]
    TAPS = i["conv_w"].shape[1]
    HIST = TAPS - 1
    DA = i["conv_w"].shape[2]
    FF = i["w_ff_up"].shape[2]
    NS = NB * NQ
    T = NS + S
    HALF = T // 2
    KT = D // P
    CT = DA // P
    QT = S // P
    TT = QT + 1
    CHUNKS = FF // D
    PAIRS = H // 2
    HQ = H * NQ
    NEWC = PAGES * PAGE
    KS = NEWC + NS
    assert (D, S, NS, H, HD, PAGE, PAGES) == (1024, 512, 32, 8, 64, 128, 2) and HQ == 32

    def tok(t):
        return (0, NS) if t == 0 else (NS + P * (t - 1), NS + P * t)

    N_GLU, N_NAT, N_OUT = 0, 8, 20
    N_FF = [28, 116]
    N_INC, N_OUTC, N_END = 92, 108, 180

    def ordinal(n):
        return n + KT + 1 if isinstance(n, int) and n < N_NAT else n - 3

    with ExitStack() as ctx:
        def sem(name):
            return ctx.enter_context(nc.semaphore(name))

        where = [nc.sbuf_base + (-nc.sbuf_base) % 64]

        def at(name, shape, dt, offset):
            return nc.alloc_sbuf_tensor_at(name, shape, dt, offset=offset)

        def room(nbytes):
            a = where[0]
            where[0] += nbytes + (-nbytes) % 32
            assert where[0] <= nc.sbuf_usable_end, where[0]
            return a

        def sb(name, shape, dt):
            n = 2 if dt == BF16 else 4
            for s in shape[1:]:
                n *= s
            return at(name, shape, dt, room(n))

        TB = T * 4
        xT = sb("xT", [P, KT, T], F32)
        reg1, reg2 = room(2 * KT * TB), room(2 * KT * TB)
        w_raw = sb("w_raw", [P, 2, KT, 256], F32)
        w_hi = sb("w_hi", [P, 4, KT, P], F32R)
        w_lo = sb("w_lo", [P, 4, KT, P], F32R)
        r_all = sb("r_all", [P, T], F32)
        zone_sq = room(3 * TB)
        zone_t = room(4 * TB)
        ident = sb("ident", [P, P], F32)
        tri = sb("tri", [P, P], F32)
        ones = sb("ones", [P, P], F32)
        ident_b = sb("ident_b", [P, P], BF16)
        mask_b = sb("mask_b", [P, P], BF16)
        maskT_b = sb("maskT_b", [NS, 2, P], BF16)
        sel = sb("sel", [H * NB, 2, P], F32)
        vec = sb("vec", [P, 60], F32)
        conv_wT = sb("conv_wT", [P, CT, 32], F32)
        qk_gain = sb("qk_gain", [P, 2, HD], F32)
        bf_b = sb("bf_b", [P, H], F32)
        eps = sb("eps", [P, 2], F32)
        r_nat = sb("r_nat", [P, TT], F32)
        wfg = sb("wfg", [P, KT, H], F32)
        f_small = sb("f_small", [P, 4, TT * H], F32)
        f_aug = sb("f_aug", [P, 2, TT * H, 2], F32)
        n_small = sb("n_small", [P, 6, 4], F32)
        soft = sb("soft", [P, 4, 4], F32)
        glu_new = sb("glu_new", [P, CT, NS], F32)
        zone_e = where[0]

        A_hi, A_lo = at("A_hi", [P, KT, T], F32R, reg1), at("A_lo", [P, KT, T], F32R, reg1 + KT * TB)
        B_hi, B_lo = at("B_hi", [P, KT, T], F32R, reg2), at("B_lo", [P, KT, T], F32R, reg2 + KT * TB)
        u_f = at("u_f", [P, KT, T], F32, reg1)
        cs_f = at("cs_f", [P, CT, T], F32, reg1 + KT * TB)
        vq_f = at("vq_f", [P, KT, T], F32, reg1 + KT * TB)
        x_nat = at("x_nat", [P, TT, D], F32, reg2)
        st_nat = at("st_nat", [P, 2, DA], F32, reg2 + TT * D * 4)
        rows = at("rows", [60, P], F32, reg2 + TT * D * 4 + 2 * DA * 4)
        cw_nat = at("cw_nat", [TAPS, DA], F32, reg2 + TT * D * 4 + 2 * DA * 4 + 512)
        qT = at("qT", [P, H, T], F32, reg2)
        c_f = at("c_f", [P, CT, T], F32, reg2 + KT * TB)
        y_nat = at("y_nat", [P, TT, D], F32, reg2)
        spare = reg2 + KT * TB + CT * TB
        ssq = at("ssq", [P, T], F32, zone_sq)
        sq = at("sq", [P, 2, T], F32, zone_sq + TB)
        prob = at("prob", [P, 2, S], F32, zone_sq)
        prob_s = at("prob_s", [P, 2, KS], F32, zone_sq)
        t_f = at("t_f", [P, 2, T], F32, zone_t)
        a_f = at("a_f", [P, 2, T], F32, zone_t + 2 * TB)
        junk = at("junk", [P, D], F32, zone_t)
        nat_raw = at("nat_raw", [P, 2, 256], F32, zone_t)
        nat_sq = at("nat_sq", [P, 2, 256], F32, zone_t + 2048)
        k_pg = at("k_pg", [P, 2, PAGES, H * HD], F32, zone_t)

        kT = sb("kT", [P, H, T], F32)
        v_nat = sb("v_nat", [P, TT, H * HD], F32)
        zone_glu = where[0]
        glu_p = sb("glu_p", [P, CT, HIST + S], F32)
        glu_s = sb("glu_s", [P, CT, NB, HIST + NQ], F32)
        zone_nb = where[0]
        nat_buf = sb("nat_buf", [P, 3, 4, HD + 2], F32)
        zone_pt = where[0]
        lf_pg = at("lf_pg", [P, PAGES, NB, H], F32, spare)
        lf_exp = at("lf_exp", [NS, NB, H], F32, spare + 512)
        spare += 768
        pT = [sb("pT0", [P, 1664], F32), at("pT1", [P, 1664], F32, spare)]
        q_bd = at("q_bd", [P, PAIRS, NB, HQ], F32, zone_pt)
        kc_T = [at("kc_T0", [P, PAIRS, NEWC], F32, zone_pt + 4096),
                at("kc_T1", [P, PAIRS, NEWC], F32, zone_sq + 8 * KS)]
        v_pg = [at(f"v_pg{s}", [P, PAGES, H * HD], F32, zone_glu + 4096 * s) for s in range(3)]
        v_pg.append(at("v_pg3", [P, PAGES, H * HD], F32, spare))
        kn_T = at("kn_T", [P, PAIRS, NS], F32, spare + 4096)
        nf_T = at("nf_T", [H * NB, KS], F32, spare + 4608)
        self_q = at("self_q", [H * NB, 2, P], F32, spare + 5760)
        at_s = at("at_s", [P, PAIRS, NS], F32, spare + 6784)
        assert 768 + 6784 + 512 <= CT * TB and 8 * KS + 4096 <= 3 * TB
        p_sT = at("p_sT", [P, 2, 3, P], F32, zone_nb)
        glu_nat = at("glu_nat", [NS, 2, DA], F32, zone_pt)
        pt_sb = at("pt_sb", [1, NB * PAGES], I32, spare + 6784)
        assert zone_pt + 8192 <= nc.sbuf_usable_end
        where[0] = zone_e
        v_f = sb("v_f", [P, KT, T], F32)
        vn_p = sb("vn_p", [P, QT, D], F32)
        vn_s = sb("vn_s", [NS, D], F32)
        ws_T = sb("ws_T", [P, H, P], F32)
        bs_b = sb("bs_b", [P, H, P], F32)
        ws4 = sb("ws4", [NS, H, NB, NQ], F32)
        ws4_r = sb("ws4_r", [NS, H, NQ], F32)
        ws_nat = at("ws_nat", [P, H, P], F32, where[0])
        rep4 = at("rep4", [NQ, NB, NQ], F32, where[0] + 4096)
        blk4 = at("blk4", [NS, NB, NQ], F32, where[0] + 4096 + 128)
        assert where[0] + 4096 + 256 <= nc.sbuf_usable_end

        V_MIX, V_FFN, V_CB, V_CG, V_CL, V_SG, V_SB = [0, 8], [16, 24], 32, 36, 40, 44, 52

        ps = ctx.enter_context(nc.psum_tensor("ps", [P, 8, 512], F32))

        def result(s):
            return ps[:, 2 * s:2 * s + 2, 0:HALF]

        def two(ap):
            return ap.rearrange("p (s c) -> p s c", s=2)

        raw_in = [sem(f"raw_in{s}") for s in range(2)]
        hi_done, lo_done, tile_done, evac_done = sem("hi_done"), sem("lo_done"), sem("tile_done"), sem("evac_done")
        nat_done, nat_evac, nat_rs, nat_sqrt = sem("nat_done"), sem("nat_evac"), sem("nat_rs"), sem("nat_sqrt")
        nat_ready, aug_done, aug_evac = sem("nat_ready"), sem("aug_done"), sem("aug_evac")
        k_stored = [sem(f"k_stored{s}") for s in range(3)]
        nat_sq_done = sem("nat_sq_done")
        xh_done, xl_done, sq_done, ssq_done = sem("xh_done"), sem("xl_done"), sem("sq_done"), sem("ssq_done")
        stat_done, sqrt_done, r_done = sem("stat_done"), sem("sqrt_done"), sem("r_done")
        ah_done, al_done, cyh_done = sem("ah_done"), sem("al_done"), sem("cyh_done")
        consts, vec_in, vec_T, vec_ok = sem("consts"), sem("vec_in"), sem("vec_T"), sem("vec_ok")
        x_in, st_in, st_T, bc_in, wfg_in, wfg_ok = sem("x_in"), sem("st_in"), sem("st_T"), sem("bc_in"), sem("wfg_in"), sem("wfg_ok")
        act_seq, dve_seq, pool_seq = sem("act_seq"), sem("dve_seq"), sem("pool_seq")
        natsq, rn_ms, rn_sqrt, rn_ok = sem("natsq"), sem("rn_ms"), sem("rn_sqrt"), sem("rn_ok")
        fg_done, z_ok, ln_ok, logf_ok = sem("fg_done"), sem("z_ok"), sem("ln_ok"), sem("logf_ok")
        fc_done, fc_ok = sem("fc_done"), sem("fc_ok")
        sig_done, glu_done, conv_done = sem("sig_done"), sem("glu_done"), sem("conv_done")
        glu_nT, glu_nat_ok = sem("glu_nT"), sem("glu_nat_ok")
        s_done, max_done, exp_done, p_ready, pT_done, pT_evac = (sem("s_done"), sem("max_done"), sem("exp_done"),
                                                                sem("p_ready"), sem("pT_done"), sem("pT_evac"))
        pv_done, mh_done, ml_done = sem("pv_done"), sem("mh_done"), sem("ml_done")
        pt_in, lf_in = sem("pt_in"), sem("lf_in")
        kpg_in = [sem(f"kpg_in{s}") for s in range(2)]
        vpg_in = [sem(f"vpg_in{s}") for s in range(4)]
        kcT_done, kcT_evac, sc_done = sem("kcT_done"), sem("kcT_evac"), sem("sc_done")
        fs_done, smp_ok, ss_done, smax_done, sexp_done, sp_ready = (sem("fs_done"), sem("smp_ok"), sem("ss_done"),
                                                                  sem("smax_done"), sem("sexp_done"), sem("sp_ready"))
        spT_done, spT_evac, spv_done = sem("spT_done"), sem("spT_evac"), sem("spv_done")
        cm_done, cx_done, cs_done, cv_done, cr_done, cy_done, cyo_done = (sem("cm_done"), sem("cx_done"), sem("cs_done"),
                                                                       sem("cv_done"), sem("cr_done"), sem("cy_done"), sem("cyo_done"))
        ws_in, ws_Tps, ws_ok, w4_ps, w4_ok, bs_in = (sem("ws_in"), sem("ws_Tps"), sem("ws_ok"), sem("w4_ps"),
                                                    sem("w4_ok"), sem("bs_in"))
        g_done, vn_T, vn_ok, mix_done, mix_ok = sem("g_done"), sem("vn_T"), sem("vn_ok"), sem("mix_done"), sem("mix_ok")
        yT_done, y_ok, stored = sem("yT_done"), sem("y_ok"), sem("stored")
        vm_done, vx_done, vs_done, vv_done, vr_done, vy_done = (sem("vm_done"), sem("vx_done"), sem("vs_done"),
                                                             sem("vv_done"), sem("vr_done"), sem("vy_done"))
        ws_masked, gm_done, vm2_done, lfe_ok, glu_stored = sem("ws_masked"), sem("gm_done"), sem("vm2_done"), sem("lfe_ok"), sem("glu_stored")

        block = ctx.enter_context(nc.Block())

        w_in = i["w_in_ab"][0].rearrange("(k p) n -> p k n", p=P)
        w_out = i["w_out_ab"][0].rearrange("(k p) n -> p k n", p=P)
        w_inc = i["w_in_c"][0].rearrange("(k p) n -> p k n", p=P)
        w_outc = i["w_out_c"][0].rearrange("(k p) n -> p k n", p=P)
        stores = [0]

        @block.sync
        def _(sp):
            def load(b, even, lo, hi):
                if not (isinstance(b, int) and b < 2):
                    sp.wait_ge(lo_done, 2 * b - 2)
                for dst, src in (lo, hi):
                    sp.dma_start(w_raw[:, even, dst[0]:dst[1], dst[2]:dst[3]], src).then_inc(raw_in[even], 16)

            def by_rows(w, c0):
                return [((4 * s, 4 * s + 4, 0, 256), w[:, 4 * s:4 * s + 4, c0:c0 + 256]) for s in range(2)]

            sp.dma_start(x_nat[0:NS, 0, :], i["x_sample"].rearrange("b q d -> (b q) d")).then_inc(x_in, 16)
            sp.dma_start(x_nat[:, 1:TT, :], i["x_prompt"][0].rearrange("(t p) d -> p t d", p=P)).then_inc(x_in, 16)
            for b in range(CT):
                load(b, b % 2, *[((0, KT, P * s, P * s + P), w_in[:, :, DA * s + P * b:DA * s + P * b + P])
                                 for s in range(2)])
            for m in range(6):
                b = N_NAT // 2 + m
                load(b, b % 2, *by_rows(w_in, 2 * DA + 256 * m))
            for m in range(4):
                b = N_OUT // 2 + m
                load(b, b % 2, *by_rows(w_out, 256 * m))

            def ffn_blocks(layer):
                up = i["w_ff_up"][layer].rearrange("(k p) n -> p k n", p=P)
                down = i["w_ff_down"][layer].rearrange("(k p) n -> p k n", p=P)
                with sp.Fori(0, CHUNKS) as c:
                    for m in range(4):
                        load(N_FF[layer] // 2 + 8 * c + m, m % 2,
                             *[((4 * s, 4 * s + 4, 0, 256),
                                up[:, 4 * s:4 * s + 4, bass.ds(c * D + 256 * m, 256)]) for s in range(2)])
                    for m in range(4):
                        load(N_FF[layer] // 2 + 8 * c + 4 + m, m % 2,
                             *[((4 * s, 4 * s + 4, 0, 256),
                                down[:, bass.ds(c * KT + 4 * s, 4), 256 * m:256 * m + 256]) for s in range(2)])

            ffn_blocks(0)
            for m in range(8):
                b = N_INC // 2 + m
                load(b, b % 2, *by_rows(w_inc, (D + 256 * m) % (2 * D)))
            for m in range(4):
                b = N_OUTC // 2 + m
                load(b, b % 2, *by_rows(w_outc, 256 * m))
            ffn_blocks(1)
            for g, (c0, c1) in enumerate(((0, 512), (512, 768), (768, 1024))):
                sp.wait_ge(y_ok, c1 // P)
                sp.dma_start(o["y_prompt"][0].rearrange("(t p) d -> p t d", p=P)[:, :, c0:c1],
                             y_nat[:, 1:TT, c0:c1]).then_inc(stored, 16)
                sp.dma_start(o["y_sample"].rearrange("b q d -> (b q) d")[:, c0:c1],
                             y_nat[0:NS, 0, c0:c1]).then_inc(stored, 16)
            sp.wait_ge(stored, 6 * 16)

        @block.gpsimd
        def _(pool):
            stored_by_pool = sem("stored_by_pool")
            n_stores = [0]

            def store(dst, src):
                pool.dma_start(dst, src).then_inc(stored_by_pool, 16)
                n_stores[0] += 1

            link = Chain(pool, pool_seq)

            def col(ap):
                return ap.rearrange("(k p) -> k p", p=P)

            for r0, src in ((V_MIX[0], i["norm_mix_g"].rearrange("l (k p) -> (l k) p", p=P)),
                            (V_FFN[0], i["norm_ffn_g"].rearrange("l (k p) -> (l k) p", p=P)),
                            (V_CB, col(i["conv_b"][0])), (V_CG, col(i["conv_ln_g"][0])),
                            (V_CL, col(i["conv_ln_b"][0])), (V_SG, col(i["sgu_ln_g"][0])),
                            (V_SB, col(i["sgu_ln_b"][0]))):
                pool.dma_start(rows[r0:r0 + src.shape[0], :], src).then_inc(vec_in, 16)
            pool.dma_start(cw_nat[:, :], i["conv_w"][0]).then_inc(vec_in, 16)
            pool.dma_start(wfg[:, :, :], w_in[:, :, 2 * DA + 3 * H * HD:]).then_inc(wfg_in, 16)
            for g in range(2):
                pool.dma_start(st_nat[0:4 * HIST, g, :],
                               i["state_conv"][0, 4 * g:4 * g + 4].rearrange("b w c -> (b w) c")).then_inc(st_in, 16)
            pool.dma_start(qk_gain[:, 0, :], i["q_norm_g"][0:1, :].broadcast_to([P, HD])).then_inc(bc_in, 16)
            pool.dma_start(qk_gain[:, 1, :], i["k_norm_g"][0:1, :].broadcast_to([P, HD])).then_inc(bc_in, 16)
            pool.dma_start(bf_b[:, :], i["b_forget"][0:1, :].broadcast_to([P, H])).then_inc(bc_in, 16)

            def mask(ap, pattern, op, base, mult, fill):
                link(pool.affine_select(out=ap, in_=ap, compare_op=op, fill=fill, base=base,
                                        pattern=pattern, channel_multiplier=mult))

            link(pool.memset(ident[:, :], 0.0))
            mask(ident[:, :], [[-1, P]], ALU.not_equal, 0, 1, 1.0)
            link(pool.memset(ones[:, :], 1.0))
            link(pool.memset(eps[:, 0:1], RMS_EPS))
            link(pool.memset(eps[:, 1:2], LN_EPS))
            pool.memset(r_nat[:, :], 1.0).then_inc(consts, 1)
            link(pool.memset(tri[:, :], 1.0))
            mask(tri[:, :], [[1, P]], ALU.is_ge, 0, -1, 0.0)
            link(pool.memset(glu_p[:, :, 0:HIST], 0.0))
            link(pool.memset(ident_b[:, :], 0.0))
            mask(ident_b[:, :], [[-1, P]], ALU.not_equal, 0, 1, 1.0)
            link(pool.memset(mask_b[:, :], 0.0))
            mask(mask_b[:, :], [[-1, P]], ALU.is_ge, 0, 1, NEG)
            link(pool.memset(maskT_b[:, :, :], 0.0))
            for g in range(2):
                m4 = maskT_b[:, g, :].rearrange("p (b h q) -> p b h q", b=4, h=H)
                mask(m4, [[-NQ, 4], [0, H], [0, NQ]], ALU.is_ge, -4 * NQ * g, 1, NEG)
                mask(m4, [[NQ, 4], [0, H], [1, NQ]], ALU.is_ge, 4 * NQ * g, -1, NEG)
            link(pool.memset(sel[:, :, :], 0.0))
            for g in range(2):
                mask(sel[:, g, :].rearrange("p (b h q) -> p b h q", b=4, h=H), [[-H, 4], [-1, H], [0, NQ]],
                     ALU.not_equal, -4 * H * g, 1, 1.0)
            pool.memset(f_aug[:, :, :, :], 1.0).then_inc(consts, 1)

            def square_sums():
                done = norm[0] * KT
                for k in range(1, KT):
                    pool.wait_ge(sq_done, done + k + 1)
                    if k > 1:
                        pool.wait_ge(ssq_done, norm[0] * (KT - 1) + k - 1)
                    pool.tensor_tensor(ssq[:, :], ssq[:, :], sq[:, k % 2, :], ALU.add).then_inc(ssq_done, 1)
                norm[0] += 1

            norm = [0]
            square_sums()

            pool.wait_ge(evac_done, KT)
            pool.dma_start(pt_sb[:, :], i["page_table"].rearrange("(a b) g -> a (b g)", a=1)).then_inc(pt_in, 16)
            pool.wait_ge(pt_in, 16)
            n_pool = i["cache_k"].shape[1]
            page = [pool.value_load(pt_sb[0:1, s:s + 1], min_val=0, max_val=n_pool - 1) for s in range(NB * PAGES)]
            lf_rows = i["cache_logf"][0].rearrange("n k h -> (n k) h")
            for b in range(NB):
                for g in range(PAGES):
                    pool.dma_start(lf_pg[:, g, b, :],
                                   lf_rows[bass.ds(page[PAGES * b + g] * PAGE, PAGE), :]).then_inc(lf_in, 16)
            pool.wait_ge(logf_ok, 1)
            logf = f_small[:, 3, :].rearrange("p (t h) -> p t h", h=H)
            store(o["logf_prompt"][0, 0].rearrange("(t p) h -> p t h", p=P), logf[:, 1:TT, :])
            store(o["logf_sample"][0].rearrange("b q h -> (b q) h"), logf[0:NS, 0, :])
            store(o["conv_sample"][0][:, 0:HIST - NQ, :], i["state_conv"][0][:, NQ:, :])
            link(pool.affine_select(out=lf_exp[:, :, :], in_=logf[0:NS, 0:1, :].broadcast_to([NS, NB, H]),
                                    compare_op=ALU.is_ge, fill=0.0, base=0, pattern=[[-NQ, NB], [0, H]],
                                    channel_multiplier=1))
            pool.affine_select(out=lf_exp[:, :, :], in_=lf_exp[:, :, :], compare_op=ALU.is_ge, fill=0.0,
                               base=NQ - 1, pattern=[[NQ, NB], [0, H]], channel_multiplier=-1).then_inc(lfe_ok, 1)
            pool.wait_ge(glu_nat_ok, 2)
            for b in range(NB):
                pool.dma_start(o["conv_sample"][0, b, HIST - NQ:, :],
                               glu_nat[NQ * b:NQ * b + NQ, 0, :]).then_inc(glu_stored, 16)
            pool.dma_start(o["conv_prompt"][0, 0], glu_nat[0:HIST, 1, :]).then_inc(glu_stored, 16)
            for m in range(2 * TT, 4 * TT):
                pool.wait_ge(nat_ready, m + 1)
                t, h0 = m % TT, 4 * (m // TT - 2)
                if t == 0:
                    dst = o["k_sample"][0].rearrange("b q h d -> (b q) h d")[:, h0:h0 + 4, :]
                    n = NS
                else:
                    dst, n = o["k_prompt"][0, 0, P * (t - 1):P * t, h0:h0 + 4, :], P
                pool.dma_start(dst, nat_buf[0:n, m % 3, :, 0:HD]).then_inc(k_stored[m % 3], 16)
            pool.wait_ge(nat_evac, 6 * TT)
            store(o["v_prompt"][0, 0].rearrange("(t p) h d -> p t (h d)", p=P), v_nat[:, 1:TT, :])
            store(o["v_sample"][0].rearrange("b q h d -> (b q) (h d)"), v_nat[0:NS, 0, :])

            def gather(cache, slot, b, arrived):
                src = cache[0].rearrange("n k h d -> (n k) (h d)")
                for g in range(PAGES):
                    pool.dma_start(slot[:, g, :], src[bass.ds(page[PAGES * b + g] * PAGE, PAGE), :]).then_inc(arrived, 16)

            def keys(b):
                if b >= 2:
                    pool.wait_ge(kcT_done, 2 * (b - 1))
                gather(i["cache_k"], k_pg[:, b % 2], b, kpg_in[b % 2])

            def vals(b):
                if b == 0:
                    pool.wait_ge(conv_done, 2 * CT * TAPS)
                    pool.wait_ge(glu_nT, 2)
                if b == 3:
                    pool.wait_ge(pv_done, H)
                if b >= 4:
                    pool.wait_ge(spv_done, b - 3)
                gather(i["cache_v"], v_pg[b % 4], b, vpg_in[b % 4])

            keys(0)
            for b in range(1, 5):
                keys(b)
                vals(b - 1)
            for b in range(5, NB):
                keys(b)
            for b in range(4, NB):
                vals(b)

            square_sums()
            pool.wait_ge(ml_done, 1)
            pool.wait_ge(tile_done, ordinal(N_OUT))
            pool.dma_start(ws_nat[:, :, :], i["w_spatial"][0].rearrange("h i j -> i h j")).then_inc(ws_in, 16)
            pool.dma_start(bs_b[:, :, :], i["b_spatial"][0:1].broadcast_to([P, H, P])).then_inc(bs_in, 16)
            link(pool.memset(rep4[:, :, :], 0.0))
            mask(rep4[:, :, :], [[0, NB], [-1, NQ]], ALU.not_equal, 0, 1, 1.0)
            link(pool.memset(blk4[:, :, :], 1.0))
            mask(blk4[:, :, :], [[-NQ, NB], [0, NQ]], ALU.is_ge, 0, 1, 0.0)
            link(pool.affine_select(out=blk4[:, :, :], in_=blk4[:, :, :], compare_op=ALU.is_ge, fill=0.0,
                                    base=NQ - 1, pattern=[[NQ, NB], [0, NQ]], channel_multiplier=-1))
            square_sums()
            pool.wait_ge(ws_Tps, 2)
            pool.wait_ge(ws_ok, 2)
            for h in range(H):
                sel_ = pool.affine_select(out=ws_T[:, h, :], in_=ws_T[:, h, :], compare_op=ALU.is_ge, fill=0.0,
                                          base=0, pattern=[[1, P]], channel_multiplier=-1)
            sel_.then_inc(ws_masked, 1)
            pool.wait_ge(vn_ok, 2 * KT)
            store(o["chunk_v"][0].rearrange("b q d -> (b q) d"), vn_s[:, :])
            square_sums()
            for s in range(3):
                pool.wait_ge(k_stored[s], 16 * len([m for m in range(2 * TT, 4 * TT) if m % 3 == s]))
            pool.wait_ge(stored_by_pool, n_stores[0] * 16)

        @block.tensor
        def _(pe):
            def tile(j, n, hi, lo, first_waits=None, k0=0, kn=KT):
                pe.wait_ge(lo_done, n + 1)
                pe.wait_ge(evac_done, ordinal(n) - 2)
                s = j % 2
                for k in range(KT):
                    if first_waits is not None:
                        first_waits(k)
                    for wt, mv, at_ in ((w_hi, hi, 0), (w_lo, hi, 1), (w_hi, lo, 2)):
                        for half in range(2):
                            mm = pe.matmul(ps[:, 2 * s + half, 0:HALF], wt[:, j % 4, k, :],
                                           mv[:, k, half * HALF:(half + 1) * HALF],
                                           start=(k == 0 and at_ == 0), stop=(k == KT - 1 and at_ == 2))
                mm.then_inc(tile_done, 1)

            def statistics(index):
                pe.wait_ge(ssq_done, (index + 1) * (KT - 1))
                for half in range(2):
                    mm = pe.matmul(ps[:, 6 + half, 0:HALF], ones[:, :], ssq[:, half * HALF:(half + 1) * HALF],
                                   start=True, stop=True)
                mm.then_inc(stat_done, 1)

            pe.wait_ge(consts, 1)
            pe.wait_ge(vec_in, 8 * 16)
            pe.transpose(ps[:, 4, 0:60], rows[:, :], ident[0:60, 0:60])
            for c in range(CT):
                mm = pe.transpose(ps[:, 5, 32 * c:32 * c + TAPS], cw_nat[:, P * c:P * c + P], ident[0:TAPS, 0:TAPS])
            mm.then_inc(vec_T, 1)
            pe.wait_ge(x_in, 32)
            for k in range(KT):
                if k >= 2:
                    pe.wait_ge(evac_done, k - 1)
                for t in range(TT):
                    n, (c0, c1) = (NS if t == 0 else P), tok(t)
                    bank, off = (0, c0) if t < 3 else (1, c0 - tok(3)[0])
                    mm = pe.transpose(ps[:, 2 * (k % 2) + bank, off:off + n], x_nat[0:n, t, P * k:P * k + P],
                                      ident[0:n, 0:n])
                mm.then_inc(tile_done, 1)
            pe.wait_ge(st_in, 32)
            for g in range(2):
                for c in range(CT):
                    mm = pe.transpose(ps[:, 6 + g, 120 * c:120 * c + 4 * HIST], st_nat[0:4 * HIST, g, P * c:P * c + P],
                                      ident[0:4 * HIST, 0:4 * HIST])
            mm.then_inc(st_T, 1)

            def forget_gates():
                pe.wait_ge(vec_ok, 2)
                pe.wait_ge(wfg_ok, 1)
                pe.wait_ge(evac_done, KT)
                for t in range(TT):
                    c0 = 0 if t == 0 else tok(t)[0]
                    for k in range(KT):
                        mm = pe.matmul(ps[:, 4, H * t:H * t + H], xT[:, k, c0:c0 + P], wfg[:, k, :],
                                       start=(k == 0), stop=(k == KT - 1))
                mm.then_inc(fg_done, 1)

            def xg_ready(index):
                return lambda k: pe.wait_ge(xl_done, KT * index + k + 1)

            for j in range(8):
                tile(j, N_GLU + j, A_hi, A_lo, xg_ready(0) if j == 0 else None)
                if j == 0:
                    pe.wait_ge(vec_ok, 4)
                    statistics(0)
                    forget_gates()
                if j == 4:
                    pe.wait_ge(logf_ok, 1)
                    pe.wait_ge(consts, 2)
                    logf = f_small[:, 3, :]
                    pe.matmul(ps[:, 5, 0:QT * H], tri[:, :], logf[:, H:TT * H], start=True, stop=False,
                              skip_group_check=True)
                    for s in range(QT - 1):
                        for t in range(s + 1, QT):
                            mm = pe.matmul(ps[:, 5, H * t:H * t + H], ones[:, :], logf[:, H * (s + 1):H * (s + 2)],
                                           start=False, stop=(s == t - 1), skip_group_check=True)
                    mm.then_inc(fc_done, 1)

            def turn_heads(m):
                t, (c0, c1) = m % TT, tok(m % TT)
                n = c1 - c0
                pe.wait_ge(nat_ready, m + 1)
                if m >= 2:
                    pe.wait_ge(aug_evac, m - 1)
                for h in range(4):
                    mm = pe.transpose(ps[0:HD + 2, 4 + m % 2, P * h:P * h + n], nat_buf[0:n, m % 3, h, :],
                                      ident[0:n, 0:n])
                mm.then_inc(aug_done, 1)

            def turn_glu():
                pe.wait_ge(glu_done, CT)
                pe.wait_ge(sqrt_done, 1)
                for c in range(CT):
                    mm = pe.transpose(ps[0:NS, 6, P * c:P * c + P], glu_new[:, c, :], ident[:, :])
                mm.then_inc(glu_nT, 1)
                for c in range(CT):
                    mm = pe.transpose(ps[0:HIST, 7, P * c:P * c + P], glu_p[:, c, S:S + HIST], ident[:, :])
                mm.then_inc(glu_nT, 1)

            pe.wait_ge(evac_done, ordinal(7))
            pe.wait_ge(fc_ok, 1)
            for m in range(6 * TT):
                blk, t = m // TT, m % TT
                if t == 0:
                    pe.wait_ge(lo_done, N_NAT + 2 * blk + 2)
                if m >= 4:
                    pe.wait_ge(nat_evac, m - 3)
                if m == 2:
                    turn_glu()
                c0 = 0 if t == 0 else tok(t)[0]
                s = (2 * blk) % 4
                for k in range(KT):
                    for wt, mv, at_ in ((w_hi, A_hi, 0), (w_lo, A_hi, 1), (w_hi, A_lo, 2)):
                        mm = pe.matmul(ps[:, m % 4, 0:256], mv[:, k, c0:c0 + P], wt[:, s:s + 2, k, :],
                                       start=(k == 0 and at_ == 0), stop=(k == KT - 1 and at_ == 2))
                mm.then_inc(nat_done, 1)
                if 2 <= m < 4 * TT + 2:
                    turn_heads(m - 2)

            def scores(s):
                h, q = s // QT, s % QT
                if s == 0:
                    pe.wait_ge(nat_evac, 6 * TT)
                    pe.wait_ge(aug_evac, 4 * TT)
                if s >= 3:
                    pe.wait_ge(exp_done, s - 2)
                n = P * (q + 1)
                pe.matmul(ps[:, s % 3, 0:n], qT[0:HD + 2, h, NS + P * q:NS + P * q + P], kT[0:HD + 2, h, NS:NS + n],
                          start=True, stop=False, skip_group_check=True)
                pe.matmul(ps[:, s % 3, P * q:n], ident_b[:, :], mask_b[:, :], start=False, stop=True,
                          skip_group_check=True).then_inc(s_done, 1)

            def turn_probs(s):
                pe.wait_ge(p_ready, s + 1)
                if s >= 3:
                    pe.wait_ge(pT_evac, s - 2)
                for j in range(s % QT + 1):
                    mm = pe.transpose(ps[:, 3 + s % 3, P * j:P * j + P], prob[:, s % 2, P * j:P * j + P], ident[:, :])
                mm.then_inc(pT_done, 1)

            def values(h):
                pe.wait_ge(pT_evac, QT * (h + 1))
                if h >= 4 and h % 2 == 0:
                    pe.wait_ge(ml_done, h // 2 - 1)
                half = HD * (h % 2)
                for j in range(QT):
                    mm = pe.matmul(ps[half:half + HD, 6 + (h // 2) % 2, P * j:S],
                                   v_nat[:, 1 + j, HD * h:HD * h + HD],
                                   pT[h % 2][:, S * j:S * j + S - P * j],
                                   start=(j == 0), stop=(j == QT - 1), skip_group_check=True)
                mm.then_inc(pv_done, 1)

            n_items = H * QT
            scores(0)
            scores(1)
            for s in range(n_items):
                if s + 2 < n_items:
                    scores(s + 2)
                turn_probs(s)
                if s % QT == 1 and s > QT:
                    values(s // QT - 1)
            values(H - 1)

            def ln_sum(src, tiles, bank, before, done):
                for k in range(tiles):
                    before(k)
                    for half in range(2):
                        mm = pe.matmul(ps[:, bank + half, 0:HALF], ones[:, :], src(k, half),
                                       start=(k == 0), stop=(k == tiles - 1), skip_group_check=True)
                    if done is not None:
                        mm.then_inc(done, 1)

            pe.wait_ge(exp_done, n_items)
            ln_sum(lambda k, half: c_f[:, k, half * HALF:(half + 1) * HALF], CT, 0,
                   lambda k: pe.wait_ge(conv_done, 2 * CT * TAPS), cm_done)

            pe.wait_ge(lf_in, NB * PAGES * 16)
            pe.wait_ge(lfe_ok, 1)
            lf0, lf1 = (lf_pg[:, g].rearrange("p b h -> p (b h)") for g in range(2))
            lfe = lf_exp[:, :, :].rearrange("p b h -> p (b h)")
            fps = ps[0:NB * H, 3, :]
            pe.wait_ge(pT_evac, n_items)
            pe.matmul(fps[:, 0:PAGE], lf0, tri[:, :], start=True, stop=True, skip_group_check=True)
            pe.matmul(fps[:, PAGE:2 * PAGE], lf1, tri[:, :], start=False, stop=False, skip_group_check=True)
            pe.matmul(fps[:, PAGE:2 * PAGE], lf0, ones[:, :], start=False, stop=False, skip_group_check=True)
            pe.matmul(fps[:, NEWC:KS], lfe, tri[0:NS, 0:NS], start=False, stop=False, skip_group_check=True)
            pe.matmul(fps[:, NEWC:KS], lf0, ones[:, 0:NS], start=False, stop=False, skip_group_check=True)
            pe.matmul(fps[:, NEWC:KS], lf1, ones[:, 0:NS], start=False, stop=True,
                      skip_group_check=True).then_inc(fs_done, 1)

            def turn_pages(b):
                pe.wait_ge(kpg_in[b % 2], 32 * (b // 2 + 1))
                for g in range(PAGES):
                    u = 2 * b + g
                    if u >= 2:
                        pe.wait_ge(kcT_evac, u - 1)
                    for p2 in range(PAIRS):
                        mm = pe.transpose(ps[:, 4 + g, P * p2:P * p2 + P], k_pg[:, b % 2, g, P * p2:P * p2 + P],
                                          ident[:, :])
                    mm.then_inc(kcT_done, 1)

            def sample_scores(b):
                g, b4 = b // 4, b % 4
                out = ps[:, 6 + g, :]
                if b4 == 0:
                    if g == 0:
                        pe.wait_ge(ml_done, PAIRS)
                        pe.wait_ge(smp_ok, 1)
                    ones_row = ones[0:NB * H, :]
                    pe.matmul(out[:, 0:KS], sel[:, g, :], nf_T[:, :], start=True, stop=False, skip_group_check=True)
                    for c0, c1 in ((0, 128), (128, 256), (256, KS)):
                        pe.matmul(out[:, c0:c1], self_q[:, g, :], ones_row[:, 0:c1 - c0], start=False, stop=False,
                                  skip_group_check=True)
                    pe.matmul(out[:, NEWC:KS], maskT_b[:, g, :], ident_b[0:NS, 0:NS], start=False, stop=False,
                              skip_group_check=True)
                    for p2 in range(PAIRS):
                        pe.matmul(out[:, NEWC:KS], q_bd[:, p2, 4 * g:4 * g + 4, :].rearrange("p b c -> p (b c)"), kn_T[:, p2, :],
                                  start=False, stop=False, skip_group_check=True)
                pe.wait_ge(kcT_evac, 2 * (b + 1))
                for p2 in range(PAIRS):
                    mm = pe.matmul(out[HQ * b4:HQ * b4 + HQ, 0:NEWC], q_bd[:, p2, b, :], kc_T[b % 2][:, p2, :],
                                   start=False, stop=(p2 == PAIRS - 1), skip_group_check=True)
                mm.then_inc(sc_done, 1)

            def turn_sample(g):
                pe.wait_ge(sp_ready, g + 1)
                out = ps[:, 3, :]
                if g == 0:
                    pe.wait_ge(smp_ok, 1)
                else:
                    pe.wait_ge(spT_evac, 1)
                pe.transpose(out[:, 0:P], prob_s[:, g, 0:P], ident[:, :])
                pe.transpose(out[:, P:2 * P], prob_s[:, g, P:2 * P], ident[:, :])
                pe.transpose(out[0:NS, 2 * P:3 * P], prob_s[:, g, NEWC:KS], ident[:, :]).then_inc(spT_done, 1)

            def sample_values(b):
                g, b4 = b // 4, b % 4
                pe.wait_ge(vpg_in[b % 4], 32 * (b // 4 + 1))
                if b4 == 0:
                    pe.wait_ge(spT_evac, g + 1)
                    if g == 0:
                        pe.wait_ge(cx_done, CT)
                for p2 in range(PAIRS):
                    out = ps[:, 2, 32 * b + 8 * p2:32 * b + 8 * p2 + 8]
                    c = HQ * b4 + 8 * p2
                    for u in range(PAGES):
                        pe.matmul(out, v_pg[b % 4][:, u, P * p2:P * p2 + P], p_sT[:, g, u, c:c + 8],
                                  start=(u == 0), stop=False, skip_group_check=True)
                    mm = pe.matmul(out, v_nat[0:NS, 0, P * p2:P * p2 + P], p_sT[0:NS, g, 2, c:c + 8],
                                   start=False, stop=True, skip_group_check=True)
                mm.then_inc(spv_done, 1)

            turn_pages(0)
            for b in range(NB):
                if b + 1 < NB:
                    turn_pages(b + 1)
                sample_scores(b)
                if b == 4:
                    ln_sum(lambda k, half: cs_f[:, k, half * HALF:(half + 1) * HALF], CT, 0,
                           lambda k: pe.wait_ge(cs_done, CT), cv_done)
                    turn_sample(0)
                if b == 5:
                    for b2 in range(2):
                        sample_values(b2)
                if b == 6:
                    for b2 in range(2, 4):
                        sample_values(b2)
            turn_sample(1)
            for b in range(4, NB):
                sample_values(b)

            pe.wait_ge(cr_done, 1)
            pe.wait_ge(mh_done, PAIRS + 1)
            for j in range(8):
                if j == 0:
                    pe.wait_ge(ml_done, PAIRS + 1)
                    pe.wait_ge(cyo_done, CT)
                tile(j, N_OUT + j, A_hi, A_lo)

            def turn_y(k):
                pe.wait_ge(evac_done, ordinal(N_END - 8 + k))
                if k == 0:
                    pe.wait_ge(sqrt_done, 4)
                if k >= 2:
                    pe.wait_ge(y_ok, k - 1)
                for t in range(1, TT):
                    pe.transpose(ps[:, 4 + k % 2, P * (t - 1):P * t], xT[:, k, tok(t)[0]:tok(t)[1]], ident[:, :])
                pe.transpose(ps[0:NS, 6 + k % 2, 0:P], xT[:, k, 0:NS], ident[:, :]).then_inc(yT_done, 1)

            def ffn_chunk(layer, c, before_up=None, after_first=None, last=False):
                n0 = N_FF[layer] + 16 * c
                for j in range(8):
                    tile(j, n0 + j, B_hi, B_lo, before_up if j == 0 else None)
                    if j == 0 and after_first is not None:
                        after_first()
                base = FFA[layer] + 8 * c
                for j in range(8):
                    tile(j, n0 + 8 + j, A_hi, A_lo,
                         (lambda k: pe.wait_ge(al_done, base + k + 1)) if j == 0 else None)
                    if last and layer == 1 and j >= 1:
                        turn_y(j - 1)
                if last and layer == 1:
                    turn_y(KT - 1)

            def ffn(layer, index):
                ffn_chunk(layer, 0, xg_ready(index), lambda: statistics(index))
                with pe.Fori(1, CHUNKS - 1) as c:
                    ffn_chunk(layer, c)
                ffn_chunk(layer, CHUNKS - 1, last=True)

            FFA = [0, 8 * CHUNKS + KT]
            ffn(0, 1)

            pe.wait_ge(ws_in, 16)
            pe.wait_ge(consts, 2)
            for h in range(H):
                mm = pe.transpose(ps[:, 4 + h // 4, P * (h % 4):P * (h % 4) + P], ws_nat[:, h, :], ident[:, :])
                if h % 4 == 3:
                    mm.then_inc(ws_Tps, 1)

            for j in range(8):
                tile(j, N_INC + j, B_hi, B_lo, xg_ready(2) if j == 0 else None)
                if j == 0:
                    statistics(2)
                if j == 2:
                    pe.wait_ge(ws_masked, 1)
                    pe.matmul(ps[0:NS, 4, 0:H * NQ], rep4[:, :, :].rearrange("p b j -> p (b j)"),
                              ws_T[0:NQ, :, 0:NQ], start=True, stop=True).then_inc(w4_ps, 1)
            for j in range(8):
                tile(j, N_INC + 8 + j, B_hi, B_lo)
                if j == 0:
                    pe.wait_ge(sqrt_done, 3)
                    ln_sum(lambda k, half: v_f[:, k, half * HALF:(half + 1) * HALF], KT, 6,
                           lambda k: pe.wait_ge(g_done, k + 1), vm_done)
                if j == 4:
                    pe.wait_ge(vx_done, KT)
                    ln_sum(lambda k, half: vq_f[:, k, half * HALF:(half + 1) * HALF], KT, 6,
                           lambda k: pe.wait_ge(vs_done, k + 1), vv_done)

            for k in range(KT):
                pe.wait_ge(vy_done, k + 1)
                if k == 0:
                    pe.wait_ge(w4_ok, 1)
                if k >= 2:
                    pe.wait_ge(vn_ok, 2 * (k - 1))
                for c in range(QT):
                    mm = pe.transpose(ps[:, 4 + k % 2, P * c:P * c + P], v_f[:, k, NS + P * c:NS + P * c + P], ident[:, :])
                mm.then_inc(vn_T, 1)
                if k == 0:
                    pe.wait_ge(vr_done, 1)
                mm = pe.transpose(ps[0:NS, 6 + k % 2, 0:P], v_f[:, k, 0:NS], ident[:, :])
                mm.then_inc(vn_T, 1)
            for h in range(H):
                pe.wait_ge(vn_ok, 2 * (h + 1))
                if h == 0:
                    pe.wait_ge(vn_ok, 2 * KT)
                if h >= 2:
                    pe.wait_ge(mix_ok, h - 1)
                for c in range(QT):
                    pe.matmul(ps[:, 4 + h % 2, P * c:P * c + P], vn_p[:, c, P * h:P * h + P], ws_T[:, h, :],
                              start=True, stop=True)
                pe.matmul(ps[:, 6 + h % 2, 0:NS], vn_s[:, P * h:P * h + P], ws4[:, h].rearrange("p b q -> p (b q)"),
                          start=True, stop=True).then_inc(mix_done, 1)
            base = 8 * CHUNKS
            for j in range(8):
                tile(j, N_OUTC + j, A_hi, A_lo, (lambda k: pe.wait_ge(al_done, base + k + 1)) if j == 0 else None)
            ffn(1, 3)

        @block.scalar
        def _(act):
            link = Chain(act, act_seq)

            def split_hi(j, n, wait=None):
                b = j // 2
                act.wait_ge(raw_in[b % 2], 32 * (n // 4 + 1) if isinstance(n, int) else wait)
                act.activation(w_hi[:, j % 4], w_raw[:, b % 2, :, P * (j % 2):P * (j % 2) + P], ACT.Copy)\
                   .then_inc(hi_done, 1)

            def round_x(k, gain, index, hi):
                act.activation(hi[:, k, :], xT[:, k, :], ACT.Copy, scale=vec[:, gain + k:gain + k + 1]).then_inc(xh_done, 1)
                if k >= 3:
                    act.wait_ge(ssq_done, index * (KT - 1) + k - 2)
                dst = ssq[:, :] if k == 0 else sq[:, k % 2, :]
                act.activation(dst, xT[:, k, :], ACT.Square).then_inc(sq_done, 1)

            def root(index):
                act.wait_ge(stat_done, index + 1)
                act.activation(two(r_all[:, :]), ps[:, 6:8, 0:HALF], ACT.Sqrt, bias=eps[:, 0:1], scale=1.0 / D)\
                   .then_inc(sqrt_done, 1)

            for n in range(2):
                split_hi(n, n)
            act.wait_ge(consts, 1)
            act.wait_ge(x_in, 32)
            for t in range(TT):
                n = NS if t == 0 else P
                link(act.activation(junk[0:n, :], x_nat[0:n, t, :], ACT.Square, accum_out=r_nat[0:n, t:t + 1]))
            act.activation(r_nat[:, :], r_nat[:, :], ACT.Sqrt, bias=eps[:, 0:1], scale=1.0 / D).then_inc(rn_sqrt, 1)
            for n in range(2, 4):
                split_hi(n, n)
            act.wait_ge(vec_ok, 1)
            for k in range(KT):
                act.wait_ge(evac_done, k + 1)
                round_x(k, V_MIX[0], 0, A_hi)
            root(0)
            act.wait_ge(z_ok, 1)
            link(act.activation(f_small[:, 1, :], f_small[:, 0, :], ACT.Abs))
            link(act.activation(f_small[:, 1, :], f_small[:, 1, :], ACT.Exp, scale=-1.0))
            act.activation(f_small[:, 2, :], f_small[:, 1, :], ACT.Ln, bias=1.0).then_inc(ln_ok, 1)

            for j in range(8):
                n = N_GLU + j
                act.wait_ge(evac_done, ordinal(n))
                if j % 2 == 1:
                    if j >= 3:
                        act.wait_ge(glu_done, j // 2)
                    act.activation(a_f[:, 0, :], t_f[:, 1, :], ACT.Sigmoid).then_inc(sig_done, 1)
                split_hi(j, n + 4)

            def nat_step(m):
                blk, t = m // TT, m % TT
                n = NS if t == 0 else P
                act.wait_ge(nat_done, m + 1)
                src = ps[0:n, m % 4, 0:256]
                if blk < 4:
                    if m >= 2:
                        act.wait_ge(nat_ready, m - 1)
                    act.activation(nat_sq[0:n, m % 2, :], src, ACT.Square, scale=r_nat[0:n, t:t + 1]).then_inc(nat_sq_done, 1)
                    act.activation(nat_raw[0:n, m % 2, :], src, ACT.Copy, scale=r_nat[0:n, t:t + 1]).then_inc(nat_evac, 1)
                else:
                    act.activation(v_nat[0:n, t, 256 * (blk - 4):256 * (blk - 3)], src, ACT.Copy,
                                   scale=r_nat[0:n, t:t + 1]).then_inc(nat_evac, 1)

            def nat_root(m):
                n = NS if m % TT == 0 else P
                act.wait_ge(nat_rs, m + 1)
                act.activation(n_small[0:n, 2 + m % 2, :], n_small[0:n, m % 2, :], ACT.Sqrt, bias=eps[0:n, 0:1],
                               scale=1.0 / HD).then_inc(nat_sqrt, 1)

            def aug_copy(m):
                t, (c0, c1) = m % TT, tok(m % TT)
                dst, h0 = (qT if m // TT < 2 else kT), 4 * (m // TT % 2)
                act.wait_ge(aug_done, m + 1)
                act.activation(dst[0:HD + 2, h0:h0 + 4, c0:c1],
                               ps[0:HD + 2, 4 + m % 2, :].rearrange("p (h c) -> p h c", h=4)[:, :, 0:c1 - c0],
                               ACT.Copy).then_inc(aug_evac, 1)

            act.wait_ge(glu_done, CT)
            for m in range(6 * TT):
                nat_step(m)
                if m < 4 * TT:
                    nat_root(m)
                if 3 <= m < 4 * TT + 3:
                    aug_copy(m - 3)
                if m == 5:
                    act.wait_ge(glu_nT, 2)
                    act.activation(glu_nat[0:NS, 0, :], ps[0:NS, 6, :], ACT.Copy).then_inc(glu_nat_ok, 1)
                    act.activation(glu_nat[0:HIST, 1, :], ps[0:HIST, 7, :], ACT.Copy).then_inc(glu_nat_ok, 1)
                if m % TT == TT - 1:
                    n = N_NAT + 2 * (m // TT)
                    split_hi(n % 4, n + 4)
                    split_hi(n % 4 + 1, n + 5)

            mx, rs = soft[:, 0, :], soft[:, 1, :]

            def exponent(s):
                n = P * (s % QT + 1)
                act.wait_ge(max_done, s + 1)
                if s >= 2:
                    act.wait_ge(pT_done, s - 1)
                act.activation(prob[:, s % 2, 0:n], ps[:, s % 3, 0:n], ACT.Exp, bias=mx[:, s % 4:s % 4 + 1],
                               accum_out=rs[:, s % 4:s % 4 + 1]).then_inc(exp_done, 1)

            def copy_probs(s):
                h, q = s // QT, s % QT
                act.wait_ge(pT_done, s + 1)
                if q == 0 and h >= 2:
                    act.wait_ge(pv_done, h - 1)
                dst = pT[h % 2][:, :].rearrange("p (j c) -> p j c", c=P)
                for_j = dst[:, q:q + 3 * q + 1:3, :] if q else dst[:, 0:1, :]
                act.activation(for_j, ps[:, 3 + s % 3, 0:P * (q + 1)].rearrange("p (j c) -> p j c", c=P), ACT.Copy)\
                   .then_inc(pT_evac, 1)

            def pair_hi(p2):
                act.wait_ge(pv_done, 2 * p2 + 2)
                act.activation(A_hi[:, CT + p2, NS:T], ps[:, 6 + p2 % 2, :], ACT.Copy).then_inc(mh_done, 1)

            act.wait_ge(glu_stored, 16 * (NB + 1))
            for s in range(H * QT):
                exponent(s)
                if s >= 1:
                    copy_probs(s - 1)
                if s % (2 * QT) == 2 and s > 2 * QT:
                    pair_hi(s // (2 * QT) - 1)
            copy_probs(H * QT - 1)
            pair_hi(PAIRS - 1)

            def conv_square(c):
                act.wait_ge(cx_done, c + 1)
                act.activation(cs_f[:, c, :], c_f[:, c, :], ACT.Square).then_inc(cs_done, 1)

            def page_copy(b, g):
                act.wait_ge(kcT_done, 2 * b + g + 1)
                if b >= 2:
                    act.wait_ge(sc_done, b - 1)
                act.activation(kc_T[b % 2][:, :, P * g:P * g + P],
                               ps[:, 4 + g, :].rearrange("p (a c) -> p a c", a=PAIRS), ACT.Copy).then_inc(kcT_evac, 1)

            def sample_exp(g):
                act.wait_ge(smax_done, g + 1)
                act.activation(prob_s[:, g, :], ps[:, 6 + g, 0:KS], ACT.Exp, bias=mx[:, g:g + 1],
                               accum_out=rs[:, g:g + 1]).then_inc(sexp_done, 1)

            def sample_copy(g):
                act.wait_ge(spT_done, g + 1)
                act.activation(p_sT[:, g, 0:2, :], ps[:, 3, 0:2 * P].rearrange("p (a c) -> p a c", a=2), ACT.Copy)
                act.activation(p_sT[0:NS, g, 2, :], ps[0:NS, 3, 2 * P:3 * P], ACT.Copy).then_inc(spT_evac, 1)

            act.wait_ge(pv_done, H)
            for b in range(NB):
                page_copy(b, 0)
                page_copy(b, 1)
                if b == 1:
                    for c in range(CT):
                        conv_square(c)
                if b == 4:
                    sample_exp(0)
                    act.wait_ge(cv_done, CT)
                    act.activation(two(r_all[:, :]), result(0), ACT.Sqrt, bias=eps[:, 1:2], scale=1.0 / DA)\
                       .then_inc(cr_done, 1)
                if b == 5:
                    sample_copy(0)
            sample_exp(1)
            sample_copy(1)
            for c in range(CT):
                act.wait_ge(cy_done, c + 1)
                link(act.activation(c_f[:, c, :], c_f[:, c, :], ACT.Silu, bias=vec[:, V_CL + c:V_CL + c + 1],
                                    scale=vec[:, V_CG + c:V_CG + c + 1]))
                act.activation(A_hi[:, c, :], c_f[:, c, :], ACT.Copy).then_inc(cyh_done, 1)
            act.wait_ge(spv_done, NB)
            att = ps[:, 2, 0:NB * HQ].rearrange("p (b a h q) -> p a h b q", b=NB, a=PAIRS, h=2)
            for half in range(2):
                rows_ = slice(HD * half, HD * half + HD)
                for p2 in range(PAIRS):
                    a_ = act.activation(at_s[rows_, p2, :].rearrange("p (b q) -> p b q", b=NB), att[rows_, p2, half], ACT.Copy)
            link(a_)
            act.activation(A_hi[:, CT:KT, 0:NS], at_s[:, :, :], ACT.Copy).then_inc(mh_done, 1)

            for j in range(8):
                n = N_OUT + j
                act.wait_ge(evac_done, ordinal(n))
                round_x(j, V_FFN[0], 1, B_hi)
                split_hi(j, n + 4)

            def ffn_chunk(layer, c, last, after_first=None):
                n0, base = N_FF[layer] + 16 * c, FFA[layer] + 8 * c
                for j in range(16):
                    n = n0 + j
                    if j == 0 and after_first is not None:
                        after_first()
                    act.wait_ge(evac_done, ordinal(n))
                    if j < 8:
                        if not (isinstance(base, int) and base + j < 2):
                            act.wait_ge(al_done, base + j - 1)
                        act.activation(a_f[:, j % 2, :], t_f[:, j % 2, :], ACT.Square)
                        act.activation(A_hi[:, j, :], t_f[:, j % 2, :], ACT.Square).then_inc(ah_done, 1)
                    elif last and layer == 0:
                        round_x(j - 8, V_MIX[1], 2, B_hi)
                    if not (isinstance(n, int) and n + 4 >= N_END):
                        split_hi(j, n + 4, 32 * ((N_FF[layer] + 4) // 4 + 4 * c + j // 4 + 1) if not isinstance(n, int) else None)
                    if last and layer == 1 and j >= 8 + 1:
                        y_copy(j - 9)

            def y_copy(k):
                act.wait_ge(yT_done, k + 1)
                act.activation(y_nat[:, 1:TT, P * k:P * k + P],
                               ps[:, 4 + k % 2, :].rearrange("p (t c) -> p t c", c=P), ACT.Copy)
                act.activation(y_nat[0:NS, 0, P * k:P * k + P], ps[0:NS, 6 + k % 2, 0:P], ACT.Copy).then_inc(y_ok, 1)

            def ffn(layer, index):
                ffn_chunk(layer, 0, False, lambda: root(index))
                with act.Fori(1, CHUNKS - 1) as c:
                    ffn_chunk(layer, c, False)
                ffn_chunk(layer, CHUNKS - 1, True)

            FFA = [0, 8 * CHUNKS + KT]
            ffn(0, 1)

            def v_square(k):
                act.wait_ge(vx_done, k + 1)
                act.activation(vq_f[:, k, :], v_f[:, k, :], ACT.Square).then_inc(vs_done, 1)

            for j in range(16):
                n = N_INC + j
                if j == 0:
                    root(2)
                act.wait_ge(evac_done, ordinal(n))
                dst = v_f[:, j, :] if j < 8 else u_f[:, j - 8, :]
                act.activation(dst, t_f[:, j % 2, :], ACT.Gelu_apprx_tanh).then_inc(g_done, 1)
                if j == 0:
                    for half in range(2):
                        act.wait_ge(ws_Tps, half + 1)
                        act.activation(ws_T[:, 4 * half:4 * half + 4, :],
                                       ps[:, 4 + half, :].rearrange("p (h c) -> p h c", h=4), ACT.Copy).then_inc(ws_ok, 1)
                split_hi(j, n + 4)
                if j == 9:
                    for k in range(4):
                        v_square(k)
                if j == 10:
                    for k in range(4, 8):
                        v_square(k)
                if j == 13:
                    act.wait_ge(vv_done, KT)
                    act.activation(two(ssq[:, :]), ps[:, 6:8, 0:HALF], ACT.Sqrt, bias=eps[:, 1:2], scale=1.0 / D)\
                       .then_inc(vr_done, 1)
                if j >= 14:
                    for k in range(4 * (j - 14), 4 * (j - 13)):
                        act.wait_ge(vm2_done, k + 1)
                        act.activation(v_f[:, k, :], v_f[:, k, :], ACT.Identity, bias=vec[:, V_SB + k:V_SB + k + 1],
                                       scale=vec[:, V_SG + k:V_SG + k + 1]).then_inc(vy_done, 1)
            for k in range(KT):
                act.wait_ge(vn_T, 2 * k + 1)
                act.activation(vn_p[:, :, P * k:P * k + P], ps[:, 4 + k % 2, :].rearrange("p (c f) -> p c f", c=QT),
                               ACT.Copy).then_inc(vn_ok, 1)
                act.wait_ge(vn_T, 2 * k + 2)
                act.activation(vn_s[:, P * k:P * k + P], ps[0:NS, 6 + k % 2, 0:P], ACT.Copy).then_inc(vn_ok, 1)
            base = 8 * CHUNKS
            for k in range(KT):
                act.wait_ge(gm_done, k + 1)
                act.activation(A_hi[:, k, :], a_f[:, k % 2, :], ACT.Copy).then_inc(ah_done, 1)
            for j in range(8):
                n = N_OUTC + j
                act.wait_ge(evac_done, ordinal(n))
                round_x(j, V_FFN[1], 3, B_hi)
                split_hi(j, n + 4)
            ffn(1, 3)
            y_copy(KT - 1)

        @block.vector
        def _(dve):
            link = Chain(dve, dve_seq)

            def evacuate_to(dst, s, r=True):
                return dve.tensor_tensor(two(dst), result(s), two(r_all[:, :]), ALU.mult)

            def split_lo(j, n):
                dve.wait_ge(hi_done, n + 1)
                dve.tensor_tensor(w_lo[:, j % 4, :, :], w_raw[:, (j // 2) % 2, :, P * (j % 2):P * (j % 2) + P],
                                  w_hi[:, j % 4, :, :].bitcast(F32), ALU.subtract).then_inc(lo_done, 1)

            def rest_x(k, gain, index, hi, lo):
                dve.wait_ge(xh_done, KT * index + k + 1)
                dve.scalar_tensor_tensor(out=lo[:, k, :], in0=xT[:, k, :], scalar=vec[:, gain + k:gain + k + 1],
                                         in1=hi[:, k, :].bitcast(F32), op0=ALU.mult, op1=ALU.subtract)\
                   .then_inc(xl_done, 1)

            def invert_r(index):
                dve.wait_ge(sqrt_done, index + 1)
                link(dve.reciprocal(r_all[:, :], r_all[:, :]))

            dve.wait_ge(vec_T, 1)
            dve.tensor_copy(vec[:, :], ps[:, 4, 0:60]).then_inc(vec_ok, 1)
            dve.tensor_copy(conv_wT[:, :, 0:TAPS], ps[:, 5, 0:32 * CT].rearrange("p (c w) -> p c w", w=32)[:, :, 0:TAPS])\
               .then_inc(vec_ok, 1)
            dve.wait_ge(vec_ok, 1)
            dve.wait_ge(wfg_in, 16)
            dve.tensor_tensor(wfg[:, :, :], wfg[:, :, :],
                              vec[:, V_MIX[0]:V_MIX[0] + KT].rearrange("p (k a) -> p k a", a=1).broadcast_to([P, KT, H]),
                              ALU.mult).then_inc(wfg_ok, 1)
            dve.wait_ge(bc_in, 48)
            link(dve.tensor_scalar(qk_gain[:, 0, :], qk_gain[:, 0, :], float(HD) ** -0.5, None, ALU.mult))
            for n in range(2):
                split_lo(n, n)
            for k in range(KT):
                dve.wait_ge(tile_done, k + 1)
                c3 = tok(3)[0]
                dve.tensor_copy(xT[:, k, 0:c3], ps[:, 2 * (k % 2), 0:c3])
                dve.tensor_copy(xT[:, k, c3:T], ps[:, 2 * (k % 2) + 1, 0:T - c3]).then_inc(evac_done, 1)
                rest_x(k, V_MIX[0], 0, A_hi, A_lo)
            split_lo(2, 2)
            dve.wait_ge(rn_sqrt, 1)
            link(dve.reciprocal(r_nat[:, :], r_nat[:, :]))
            dve.wait_ge(st_T, 1)
            for g in range(2):
                for c in range(CT):
                    cp = dve.tensor_copy(glu_s[:, c, 4 * g:4 * g + 4, 0:HIST],
                                         ps[:, 6 + g, 120 * c:120 * c + 4 * HIST].rearrange("p (b w) -> p b w", b=4))
                cp.then_inc(vec_ok, 1)

            def gates():
                dve.wait_ge(fg_done, 1)
                for t in range(TT):
                    z = dve.scalar_tensor_tensor(out=f_small[:, 0, H * t:H * t + H], in0=ps[:, 4, H * t:H * t + H],
                                                 scalar=r_nat[:, t:t + 1], in1=bf_b[:, :], op0=ALU.mult, op1=ALU.add)
                z.then_inc(z_ok, 1)
                dve.wait_ge(ln_ok, 1)
                dve.scalar_tensor_tensor(out=f_small[:, 3, :], in0=f_small[:, 0, :], scalar=0.0, in1=f_small[:, 2, :],
                                         op0=ALU.min, op1=ALU.subtract).then_inc(logf_ok, 1)

            for j in range(8):
                n = N_GLU + j
                if j == 0:
                    invert_r(0)
                dve.wait_ge(tile_done, ordinal(n))
                if j >= 2:
                    dve.wait_ge(glu_done, j // 2)
                evacuate_to(t_f[:, j % 2, :], j % 2).then_inc(evac_done, 1)
                split_lo(j + 3, n + 3)
                if j == 0:
                    gates()
                if j % 2 == 1:
                    c = j // 2
                    dve.wait_ge(sig_done, c + 1)
                    dve.tensor_tensor(glu_p[:, c, HIST:HIST + S], t_f[:, 0, NS:T], a_f[:, 0, NS:T], ALU.mult)
                    dve.tensor_tensor(glu_s[:, c, :, HIST:HIST + NQ],
                                      t_f[:, 0, 0:NS].rearrange("p (b q) -> p b q", b=NB),
                                      a_f[:, 0, 0:NS].rearrange("p (b q) -> p b q", b=NB), ALU.mult)
                    dve.tensor_tensor(glu_new[:, c, :], t_f[:, 0, 0:NS], a_f[:, 0, 0:NS], ALU.mult).then_inc(glu_done, 1)
                if j == 5:
                    dve.wait_ge(fc_done, 1)
                    dve.wait_ge(consts, 2)
                    dve.tensor_copy(f_aug[:, 0, H:TT * H, 0], ps[:, 5, 0:QT * H])
                    dve.tensor_scalar(f_aug[:, 1, H:TT * H, 1], ps[:, 5, 0:QT * H], -1.0, None, ALU.mult)\
                       .then_inc(fc_ok, 1)

            def conv(u0, u1):
                for u in range(u0, min(u1, 2 * CT * TAPS)):
                    tap, c, sampled = u // (2 * CT), (u // 2) % CT, u % 2
                    if u >= 2 * CT:
                        dve.wait_ge(conv_done, u - 2 * CT + 1)
                    if sampled:
                        src = glu_s[:, c, :, tap:tap + NQ]
                        dst = c_f[:, c, 0:NS].rearrange("p (b q) -> p b q", b=NB)
                    else:
                        src, dst = glu_p[:, c, tap:tap + S], c_f[:, c, NS:T]
                    if tap == 0:
                        dve.tensor_scalar(dst, src, conv_wT[:, c, 0:1], vec[:, V_CB + c:V_CB + c + 1], ALU.mult,
                                          ALU.add).then_inc(conv_done, 1)
                    else:
                        dve.scalar_tensor_tensor(out=dst, in0=src, scalar=conv_wT[:, c, tap:tap + 1], in1=dst,
                                                 op0=ALU.mult, op1=ALU.add).then_inc(conv_done, 1)

            def sums(m):
                n = NS if m % TT == 0 else P
                dve.wait_ge(nat_sq_done, m + 1)
                dve.tensor_reduce(n_small[0:n, m % 2, :], nat_sq[0:n, m % 2, :].rearrange("p (h d) -> p h d", h=4),
                                  AX_X, ALU.add).then_inc(nat_rs, 1)

            def normalise(m):
                blk, t = m // TT, m % TT
                n = NS if t == 0 else P
                buf, head = nat_buf[0:n, m % 3], n_small[0:n, 4 + m % 2, :]
                dve.wait_ge(nat_sqrt, m + 1)
                link(dve.reciprocal(head, n_small[0:n, 2 + m % 2, :]))
                dve.wait_ge(nat_evac, m + 1)
                if m >= 3:
                    dve.wait_ge(aug_done, m - 2)
                    if m - 3 >= 2 * TT:
                        dve.wait_ge(k_stored[m % 3], 16 * len([u for u in range(2 * TT, m - 2) if u % 3 == m % 3]))
                link(dve.tensor_tensor(buf[:, :, 0:HD], nat_raw[0:n, m % 2, :].rearrange("p (h d) -> p h d", h=4),
                                       head.rearrange("p (h a) -> p h a", a=1).broadcast_to([n, 4, HD]), ALU.mult))
                dve.tensor_copy(buf[:, :, HD:HD + 2],
                                f_aug[0:n, blk // 2, H * t + 4 * (blk % 2):H * t + 4 * (blk % 2) + 4, :])
                dve.tensor_tensor(buf[:, :, 0:HD], buf[:, :, 0:HD],
                                  qk_gain[0:n, blk // 2:blk // 2 + 1, :].broadcast_to([n, 4, HD]), ALU.mult)\
                   .then_inc(nat_ready, 1)

            split_lo(11, 11)
            dve.wait_ge(glu_done, CT)
            dve.wait_ge(fc_ok, 1)
            cu = 0
            for m in range(6 * TT):
                if m < 4 * TT:
                    sums(m)
                if 1 <= m < 4 * TT + 1:
                    normalise(m - 1)
                if m % TT == 1 and m > TT:
                    n = N_NAT + 2 * (m // TT - 1) + 4
                    split_lo(n, n)
                    split_lo(n + 1, n + 1)
                conv(cu, cu + CONV_NAT)
                cu += CONV_NAT
            split_lo(N_OUT + 2, N_OUT + 2)

            mx, rs, ri = soft[:, 0, :], soft[:, 1, :], soft[:, 2, :]

            def maximum(s):
                dve.wait_ge(s_done, s + 1)
                dve.tensor_reduce(mx[:, s % 4:s % 4 + 1], ps[:, s % 3, 0:P * (s % QT + 1)], AX_X, ALU.max,
                                  negate=True).then_inc(max_done, 1)

            def share(s):
                dve.wait_ge(exp_done, s + 1)
                link(dve.reciprocal(ri[:, s % 4:s % 4 + 1], rs[:, s % 4:s % 4 + 1]))
                n = P * (s % QT + 1)
                dve.tensor_scalar(prob[:, s % 2, 0:n], prob[:, s % 2, 0:n], ri[:, s % 4:s % 4 + 1], None, ALU.mult)\
                   .then_inc(p_ready, 1)

            def pair_lo(p2):
                dve.wait_ge(mh_done, p2 + 1)
                dve.tensor_tensor(A_lo[:, CT + p2, NS:T], ps[:, 6 + p2 % 2, :], A_hi[:, CT + p2, NS:T].bitcast(F32),
                                  ALU.subtract).then_inc(ml_done, 1)

            for s in range(H * QT):
                maximum(s)
                if s >= 1:
                    share(s - 1)
                if s % (2 * QT) == 3 and s > 2 * QT:
                    pair_lo(s // (2 * QT) - 1)
                conv(cu, cu + CONV_ATT)
                cu += CONV_ATT
            share(H * QT - 1)
            conv(cu, 2 * CT * TAPS)
            pair_lo(PAIRS - 1)

            dve.wait_ge(pv_done, H)
            dve.wait_ge(pT_evac, H * QT)
            link(dve.memset(q_bd[:, :, :, :], 0.0))
            for h in range(H):
                rows_ = slice(HD * (h % 2), HD * (h % 2) + HD)
                dve.tensor_copy(q_bd[rows_, h // 2, :, NQ * h:NQ * h + NQ],
                                qT[0:HD, h, 0:NS].rearrange("p (b q) -> p b q", b=NB))
                dve.tensor_copy(kn_T[rows_, h // 2, :], kT[0:HD, h, 0:NS])
            dve.wait_ge(fs_done, 1)
            dve.tensor_scalar(nf_T[:, :], ps[0:NB * H, 3, 0:KS], -1.0, None, ALU.mult)
            for g in range(2):
                c0 = NEWC + 4 * NQ * g
                f_q = ps[0:NB * H, 3, c0:c0 + 4 * NQ].rearrange("p (b a q) -> p b a q", b=4, a=1)
                cp = dve.tensor_tensor(self_q[:, g, :].rearrange("p (b h q) -> p b h q", b=4, h=H),
                                       f_q.broadcast_to([NB * H, 4, H, NQ]),
                                       sel[:, g, :].rearrange("p (b h q) -> p b h q", b=4, h=H), ALU.mult)
            cp.then_inc(smp_ok, 1)

            dve.wait_ge(cm_done, CT)
            for c in range(CT):
                dve.scalar_tensor_tensor(out=two(c_f[:, c, :]), in0=result(0), scalar=-1.0 / DA, in1=two(c_f[:, c, :]),
                                         op0=ALU.mult, op1=ALU.add).then_inc(cx_done, 1)

            def sample_max(g):
                dve.wait_ge(ss_ready, SCORES[g])
                dve.tensor_reduce(mx[:, g:g + 1], ps[:, 6 + g, 0:KS], AX_X, ALU.max, negate=True).then_inc(smax_done, 1)

            def sample_share(g):
                dve.wait_ge(sexp_done, g + 1)
                link(dve.reciprocal(ri[:, g:g + 1], rs[:, g:g + 1]))
                dve.tensor_scalar(prob_s[:, g, :], prob_s[:, g, :], ri[:, g:g + 1], None, ALU.mult).then_inc(sp_ready, 1)

            ss_ready, SCORES = sc_done, [4, 8]
            sample_max(0)
            sample_share(0)
            dve.wait_ge(cr_done, 1)
            link(dve.reciprocal(r_all[:, :], r_all[:, :]))
            for c in range(CT):
                dve.tensor_tensor(c_f[:, c, :], c_f[:, c, :], r_all[:, :], ALU.mult).then_inc(cy_done, 1)
            sample_max(1)
            sample_share(1)
            for c in range(CT):
                dve.wait_ge(cyh_done, c + 1)
                dve.tensor_tensor(A_lo[:, c, :], c_f[:, c, :], A_hi[:, c, :].bitcast(F32), ALU.subtract).then_inc(cyo_done, 1)
            dve.wait_ge(mh_done, PAIRS + 1)
            dve.tensor_tensor(A_lo[:, CT:KT, 0:NS], at_s[:, :, :], A_hi[:, CT:KT, 0:NS].bitcast(F32), ALU.subtract)\
               .then_inc(ml_done, 1)

            def add_to_x(k, n, s):
                dve.wait_ge(tile_done, ordinal(n))
                dve.tensor_tensor(two(xT[:, k, :]), result(s), two(xT[:, k, :]), ALU.add).then_inc(evac_done, 1)

            for j in range(8):
                n = N_OUT + j
                add_to_x(j, n, j % 2)
                split_lo(j + 3, n + 3)
                rest_x(j, V_FFN[0], 1, B_hi, B_lo)

            FFA = [0, 8 * CHUNKS + KT]

            def ffn_chunk(layer, c, last, before_first=None):
                n0, base = N_FF[layer] + 16 * c, FFA[layer] + 8 * c
                if before_first is not None:
                    before_first()
                for j in range(16):
                    n = n0 + j
                    if j < 8:
                        dve.wait_ge(tile_done, ordinal(n))
                        if not (isinstance(base, int) and base + j < 2):
                            dve.wait_ge(ah_done, base + j - 1)
                        dve.scalar_tensor_tensor(out=two(t_f[:, j % 2, :]), in0=result(j % 2), scalar=0.0,
                                                 in1=two(r_all[:, :]), op0=ALU.max, op1=ALU.mult).then_inc(evac_done, 1)
                    else:
                        add_to_x(j - 8, n, j % 2)
                    if not (isinstance(n, int) and n + 3 >= N_END):
                        split_lo(j + 3, n + 3)
                    if j < 8:
                        dve.wait_ge(ah_done, base + j + 1)
                        dve.tensor_tensor(A_lo[:, j, :], a_f[:, j % 2, :], A_hi[:, j, :].bitcast(F32), ALU.subtract)\
                           .then_inc(al_done, 1)
                    elif last and layer == 0:
                        rest_x(j - 8, V_MIX[1], 2, B_hi, B_lo)

            def ffn(layer, index):
                ffn_chunk(layer, 0, False, lambda: invert_r(index))
                with dve.Fori(1, CHUNKS - 1) as c:
                    ffn_chunk(layer, c, False)
                ffn_chunk(layer, CHUNKS - 1, True)

            ffn(0, 1)

            for j in range(16):
                n = N_INC + j
                if j == 0:
                    invert_r(2)
                dve.wait_ge(tile_done, ordinal(n))
                if j >= 2:
                    dve.wait_ge(g_done, j - 1)
                evacuate_to(t_f[:, j % 2, :], j % 2).then_inc(evac_done, 1)
                split_lo(j + 3, n + 3)
                if j == 4:
                    dve.wait_ge(w4_ps, 1)
                    w4 = ps[0:NS, 4, 0:H * NQ].rearrange("p (h a q) -> p h a q", h=H, a=1).broadcast_to([NS, H, NB, NQ])
                    dve.tensor_tensor(ws4[:, :, :, :], w4,
                                      blk4[:, :, :].rearrange("p (a b) q -> p a b q", a=1).broadcast_to([NS, H, NB, NQ]),
                                      ALU.mult).then_inc(w4_ok, 1)
                if j == 9:
                    dve.wait_ge(vm_done, KT)
                    for k in range(KT):
                        dve.scalar_tensor_tensor(out=two(v_f[:, k, :]), in0=ps[:, 6:8, 0:HALF], scalar=-1.0 / D,
                                                 in1=two(v_f[:, k, :]), op0=ALU.mult, op1=ALU.add).then_inc(vx_done, 1)
                if j == 14:
                    dve.wait_ge(vr_done, 1)
                    link(dve.reciprocal(ssq[:, :], ssq[:, :]))
                if j >= 14:
                    for k in range(4 * (j - 14), 4 * (j - 13)):
                        dve.tensor_tensor(v_f[:, k, :], v_f[:, k, :], ssq[:, :], ALU.mult).then_inc(vm2_done, 1)

            base = 8 * CHUNKS
            dve.wait_ge(g_done, 16)
            dve.wait_ge(bs_in, 16)
            for h in range(H):
                dve.wait_ge(mix_done, h + 1)
                dve.tensor_tensor(v_f[:, h, NS:T].rearrange("p (c q) -> p c q", c=QT),
                                  ps[:, 4 + h % 2, :].rearrange("p (c q) -> p c q", c=QT),
                                  bs_b[:, h:h + 1, :].broadcast_to([P, QT, P]), ALU.add)
                dve.tensor_tensor(v_f[:, h, 0:NS].rearrange("p (b q) -> p b q", b=NB),
                                  ps[:, 6 + h % 2, 0:NS].rearrange("p (b q) -> p b q", b=NB),
                                  bs_b[:, h:h + 1, 0:NQ].broadcast_to([P, NB, NQ]), ALU.add).then_inc(mix_ok, 1)
                dve.wait_ge(mix_ok, h + 1)
                dve.tensor_tensor(a_f[:, h % 2, :], u_f[:, h, :], v_f[:, h, :], ALU.mult).then_inc(gm_done, 1)
                dve.wait_ge(ah_done, base + h + 1)
                dve.tensor_tensor(A_lo[:, h, :], a_f[:, h % 2, :], A_hi[:, h, :].bitcast(F32), ALU.subtract)\
                   .then_inc(al_done, 1)
            for j in range(8):
                n = N_OUTC + j
                add_to_x(j, n, j % 2)
                split_lo(j + 3, n + 3)
                rest_x(j, V_FFN[1], 3, B_hi, B_lo)
            ffn(1, 3)


CONV_NAT, CONV_ATT = 5, 3


def kernel(**inputs):
    import numpy as np
    import concourse.bacc as bacc
    from concourse.bass_utils import run_bass_kernel_spmd

    nc = bacc.Bacc("TRN2", target_bir_lowering=False, num_devices=1)
    arrays, ins, outs = {}, {}, {}
    for name in INPUTS:
        a = np.ascontiguousarray(inputs[name])
        arrays[f"in_{name}"] = a
        ins[name] = nc.dram_tensor(f"in_{name}", a.shape, mybir.dt.from_np(a.dtype), kind="ExternalInput").ap()
    shapes = output_shapes({name: inputs[name].shape for name in INPUTS})
    for name, shape in shapes:
        outs[name] = nc.dram_tensor(f"out_{name}", shape, F32, kind="ExternalOutput").ap()
    build(nc, ins, outs)
    r = run_bass_kernel_spmd(nc, [arrays], core_ids=[0])
    return tuple(r.results[0][f"out_{name}"] for name, _ in shapes)
```

```python
from contextlib import ExitStack

import concourse.bass as bass
from concourse import mybir

F32 = mybir.dt.float32
F32R = mybir.dt.float32r
BF16 = mybir.dt.bfloat16
I32 = mybir.dt.int32
ACT = mybir.ActivationFunctionType
ALU = mybir.AluOpType
AX_X = mybir.AxisListType.X

CONV_GLU, CONV_QK, CONV_V, CONV_ATT = 3, 3, 3, 2
LN_MEAN, LN_VAR = 19, 26

SGU_VAR = 3

P = 128
NEG = -1.0e30
RMS_EPS = 1e-6
LN_EPS = 1e-5

INPUTS = ["x_prompt", "x_sample", "cache_k", "cache_v", "cache_logf", "state_conv", "page_table",
          "norm_mix_g", "norm_ffn_g", "w_in_ab", "b_forget", "q_norm_g", "k_norm_g", "conv_w",
          "conv_b", "conv_ln_g", "conv_ln_b", "w_out_ab", "w_in_c", "sgu_ln_g", "sgu_ln_b",
          "w_spatial", "b_spatial", "w_out_c", "w_ff_up", "w_ff_down"]


def output_shapes(a):
    batch, seq, d = a["x_prompt"]
    nb, nq, _ = a["x_sample"]
    nab, _, _, heads, hd = a["cache_k"]
    hist, da = a["state_conv"][2:]
    nc_layers = a["w_in_c"][0]
    return [("y_prompt", (batch, seq, d)), ("y_sample", (nb, nq, d)),
            ("k_prompt", (nab, batch, seq, heads, hd)), ("v_prompt", (nab, batch, seq, heads, hd)),
            ("logf_prompt", (nab, batch, seq, heads)),
            ("k_sample", (nab, nb, nq, heads, hd)), ("v_sample", (nab, nb, nq, heads, hd)),
            ("logf_sample", (nab, nb, nq, heads)),
            ("conv_prompt", (nab, batch, hist, da)), ("conv_sample", (nab, nb, hist, da)),
            ("chunk_v", (nc_layers, nb, nq, d))]


class Chain:

    def __init__(self, engine, sem):
        self.engine, self.sem, self.count = engine, sem, 0

    def __call__(self, instruction):
        self.count += 1
        instruction.then_inc(self.sem, 1)
        self.engine.wait_ge(self.sem, self.count)


def build(nc, i, o):
    D = i["x_prompt"].shape[2]
    S = i["x_prompt"].shape[1]
    NB, NQ, _ = i["x_sample"].shape
    H, HD = i["cache_k"].shape[3:]
    PAGE = i["cache_k"].shape[2]
    PAGES = i["page_table"].shape[1]
    TAPS = i["conv_w"].shape[1]
    HIST = TAPS - 1
    DA = i["conv_w"].shape[2]
    FF = i["w_ff_up"].shape[2]
    NS = NB * NQ
    T = NS + S
    HALF = T // 2
    KT = D // P
    CT = DA // P
    QT = S // P
    TT = QT + 1
    CHUNKS = FF // D
    PAIRS = H // 2
    HQ = H * NQ
    NEWC = PAGES * PAGE
    KS = NEWC + NS
    assert (D, S, NS, H, HD, PAGE, PAGES) == (1024, 512, 32, 8, 64, 128, 2) and HQ == 32

    def tok(t):
        return (0, NS) if t == 0 else (NS + P * (t - 1), NS + P * t)

    N_GLU, N_NAT, N_OUT = 0, 8, 20
    N_FF = [28, 116]
    N_INC, N_OUTC, N_END = 92, 108, 180

    def ordinal(n):
        return n + KT + 1 if isinstance(n, int) and n < N_NAT else n - 3

    with ExitStack() as ctx:
        def sem(name):
            return ctx.enter_context(nc.semaphore(name))

        where = [nc.sbuf_base + (-nc.sbuf_base) % 64]

        def at(name, shape, dt, offset):
            return nc.alloc_sbuf_tensor_at(name, shape, dt, offset=offset)

        def room(nbytes):
            a = where[0]
            where[0] += nbytes + (-nbytes) % 32
            assert where[0] <= nc.sbuf_usable_end, where[0]
            return a

        def sb(name, shape, dt):
            n = 2 if dt == BF16 else 4
            for s in shape[1:]:
                n *= s
            return at(name, shape, dt, room(n))

        TB = T * 4
        xT = sb("xT", [P, KT, T], F32)
        reg1, reg2 = room(2 * KT * TB), room(2 * KT * TB)
        w_raw = sb("w_raw", [P, 2, KT, 256], F32)
        w_hi = sb("w_hi", [P, 4, KT, P], F32R)
        w_lo = sb("w_lo", [P, 4, KT, P], F32R)
        r_all = sb("r_all", [P, T], F32)
        zone_sq = room(3 * TB)
        zone_t = room(4 * TB)
        ident = sb("ident", [P, P], F32)
        tri = sb("tri", [P, P], F32)
        ones = sb("ones", [P, P], F32)
        ident_b = sb("ident_b", [P, P], BF16)
        mask_b = sb("mask_b", [P, P], BF16)
        maskT_b = sb("maskT_b", [NS, 2, P], BF16)
        head_is = sb("head_is", [P, H], F32)
        heads = sb("heads", [P, 4, H], F32)
        sel = sb("sel", [H * NB, 2, P], F32)
        vec = sb("vec", [P, 60], F32)
        conv_wT = sb("conv_wT", [P, CT, 32], F32)
        qk_gain = sb("qk_gain", [P, 2, HD], F32)
        bf_c = sb("bf_c", [H, 1], F32)
        eps = sb("eps", [P, 2], F32)
        r_nat = sb("r_nat", [P, TT], F32)
        f_small = sb("f_small", [P, TT * H], F32)
        f_aug = sb("f_aug", [P, 2, TT * H, 2], F32)
        n_small = sb("n_small", [P, 6, 4], F32)
        soft = sb("soft", [P, 4, 4], F32)
        glu_new = sb("glu_new", [P, CT, NS], F32)
        zone_e = where[0]

        A_hi, A_lo = at("A_hi", [P, KT, T], F32R, reg1), at("A_lo", [P, KT, T], F32R, reg1 + KT * TB)
        B_hi, B_lo = at("B_hi", [P, KT, T], F32R, reg2), at("B_lo", [P, KT, T], F32R, reg2 + KT * TB)
        u_f = at("u_f", [P, KT, T], F32, reg1)
        cs_f = at("cs_f", [P, CT, T], F32, reg1 + KT * TB)
        vq_f = at("vq_f", [P, KT, T], F32, reg1 + KT * TB)
        x_nat = at("x_nat", [P, TT, D], F32, reg2)
        st_nat = at("st_nat", [P, 2, DA], F32, reg2 + TT * D * 4)
        rows = at("rows", [60, P], F32, reg2 + TT * D * 4 + 2 * DA * 4)
        cw_nat = at("cw_nat", [TAPS, DA], F32, reg2 + TT * D * 4 + 2 * DA * 4 + 512)
        qT = at("qT", [P, H, T], F32, reg2)
        c_f = at("c_f", [P, CT, T], F32, reg2 + KT * TB)
        y_nat = at("y_nat", [P, TT, D], F32, reg2)
        spare = reg2 + KT * TB + CT * TB
        ssq = at("ssq", [P, T], F32, zone_sq)
        sq = at("sq", [P, 2, T], F32, zone_sq + TB)
        prob = at("prob", [P, 2, S], F32, zone_sq)
        prob_s = at("prob_s", [P, 2, KS], F32, zone_sq)
        t_f = at("t_f", [P, 2, T], F32, zone_t)
        a_f = at("a_f", [P, 2, T], F32, zone_t + 2 * TB)
        junk = at("junk", [P, D], F32, zone_t)
        nat_raw = at("nat_raw", [P, 2, 256], F32, zone_t)
        nat_sq = at("nat_sq", [P, 2, 256], F32, zone_t + 2048)
        k_pg = at("k_pg", [P, 2, PAGES, H * HD], F32, zone_t)

        zone_kT = where[0]
        kT = sb("kT", [P, H, T], F32)
        v_nat = sb("v_nat", [P, TT, H * HD], F32)
        zone_glu = where[0]
        glu_p = sb("glu_p", [P, CT, HIST + S], F32)
        glu_s = sb("glu_s", [P, CT, NB, HIST + NQ], F32)
        zone_nb = where[0]
        nat_buf = sb("nat_buf", [P, 3, 4, HD + 2], F32)
        zone_pt = where[0]
        lf_pg = at("lf_pg", [P, PAGES, NB, H], F32, spare)
        lf_exp = at("lf_exp", [NS, NB, H], F32, spare + 512)
        spare += 768
        pT = [sb("pT0", [P, 1664], F32), at("pT1", [P, 1664], F32, spare)]
        wf_raw = at("wf_raw", [P, KT, P], F32, zone_kT)
        wf_hi = at("wf_hi", [P, KT, P], F32R, zone_kT + 4096)
        wf_lo = at("wf_lo", [P, KT, P], F32R, zone_kT + 8192)
        gate = at("gate", [H, 4, T], F32, zone_kT + 12288)
        q_bd = at("q_bd", [P, PAIRS, NB, HQ], F32, reg1)
        kn_T = at("kn_T", [P, PAIRS, NS], F32, reg1 + 4096)
        nf_T = at("nf_T", [H * NB, KS], F32, reg1 + 4608)
        self_q = at("self_q", [H * NB, 2, P], F32, reg1 + 5760)
        assert 6784 <= CT * TB
        kc_T = [at(f"kc_T{s}", [P, PAIRS, NEWC], F32, zone_glu + 4096 * s) for s in range(2)]
        v_pg = [at(f"v_pg{b}", [P, PAGES, H * HD], F32, (zone_kT if b < 4 else reg2) + (b % 4) * 2 * TB)
                for b in range(NB)]
        prod = [at(f"prod{s}", [P, NB, NQ, TAPS], F32, spare + 4 * NS * TAPS * s) for s in range(2)]
        at_s = at("at_s", [P, PAIRS, NS], F32, zone_sq + 8 * KS)
        own = at("own", [P, 2, H * HD], F32, zone_t)
        assert 768 + 8 * NS * TAPS <= CT * TB and 8 * KS + 512 <= 3 * TB
        p_sT = at("p_sT", [P, 2, 3, P], F32, zone_nb)
        glu_nat = at("glu_nat", [NS, 2, DA], F32, zone_pt)
        pt_sb = at("pt_sb", [1, NB * PAGES], I32, zone_pt + 8192 - 64 - 1536)
        assert zone_pt + 6656 <= nc.sbuf_usable_end
        where[0] = zone_e
        v_f = sb("v_f", [P, KT, T], F32)
        vn_p = sb("vn_p", [P, QT, D], F32)
        vn_s = sb("vn_s", [NS, D], F32)
        ws_T = sb("ws_T", [P, H, P], F32)
        bs_b = sb("bs_b", [P, H, P], F32)
        ws4 = sb("ws4", [NS, H, NB, NQ], F32)
        ws4_r = sb("ws4_r", [NS, H, NQ], F32)
        ws_nat = at("ws_nat", [P, H, P], F32, where[0])
        rep4 = at("rep4", [NQ, NB, NQ], F32, where[0] + 4096)
        blk4 = at("blk4", [NS, NB, NQ], F32, where[0] + 4096 + 128)
        assert where[0] + 4096 + 256 <= nc.sbuf_usable_end

        V_MIX, V_FFN, V_CB, V_CG, V_CL, V_SG, V_SB = [0, 8], [16, 24], 32, 36, 40, 44, 52

        ps = ctx.enter_context(nc.psum_tensor("ps", [P, 8, 512], F32))

        def result(s):
            return ps[:, 2 * s:2 * s + 2, 0:HALF]

        def glu_window(c):
            rows_ = glu_s[:, c, :, :]
            return bass.AP(rows_.tensor, rows_.offset, [list(rows_.ap[0]), [HIST + NQ, NB], [1, NQ], [1, TAPS]])

        def two(ap):
            return ap.rearrange("p (s c) -> p s c", s=2)

        raw_in = [sem(f"raw_in{s}") for s in range(2)]
        hi_done, lo_done, tile_done, evac_done = sem("hi_done"), sem("lo_done"), sem("tile_done"), sem("evac_done")
        nat_done, nat_evac, nat_rs, nat_sqrt = sem("nat_done"), sem("nat_evac"), sem("nat_rs"), sem("nat_sqrt")
        nat_ready, aug_done, aug_evac = sem("nat_ready"), sem("aug_done"), sem("aug_evac")
        k_stored = [sem(f"k_stored{s}") for s in range(3)]
        nat_sq_done = sem("nat_sq_done")
        xh_done, xl_done, sq_done, ssq_done = sem("xh_done"), sem("xl_done"), sem("sq_done"), sem("ssq_done")
        stat_done, sqrt_done, r_done = sem("stat_done"), sem("sqrt_done"), sem("r_done")
        ah_done, al_done, cyh_done = sem("ah_done"), sem("al_done"), sem("cyh_done")
        consts, vec_in, vec_T, vec_ok = sem("consts"), sem("vec_in"), sem("vec_T"), sem("vec_ok")
        st_in, st_T, bc_in, wfg_in, wfg_ok = sem("st_in"), sem("st_T"), sem("bc_in"), sem("wfg_in"), sem("wfg_ok")
        x_in = [sem(f"x_in{g}") for g in range(4)]
        xc_done, prod_done, psum_red, bd_zero, prep_done, silu_done = (sem("xc_done"), sem("prod_done"), sem("psum_red"),
                                                                   sem("bd_zero"), sem("prep_done"), sem("silu_done"))
        act_seq, dve_seq, pool_seq = sem("act_seq"), sem("dve_seq"), sem("pool_seq")
        natsq, rn_ms, rn_sqrt, rn_ok = sem("natsq"), sem("rn_ms"), sem("rn_sqrt"), sem("rn_ok")
        logT_ok, log_T, fg_done, z_ok, ln_ok, logf_ok = sem("logT_ok"), sem("log_T"), sem("fg_done"), sem("z_ok"), sem("ln_ok"), sem("logf_ok")
        fc_done, fc_ok = sem("fc_done"), sem("fc_ok")
        sig_done, glu_done, conv_done = sem("sig_done"), sem("glu_done"), sem("conv_done")
        glu_nT, glu_nat_ok = sem("glu_nT"), sem("glu_nat_ok")
        s_done, max_done, exp_done, p_ready, pT_done, pT_evac = (sem("s_done"), sem("max_done"), sem("exp_done"),
                                                                sem("p_ready"), sem("pT_done"), sem("pT_evac"))
        pv_done, mh_done, ml_done = sem("pv_done"), sem("mh_done"), sem("ml_done")
        pt_in, lf_in = sem("pt_in"), sem("lf_in")
        kpg_in = [sem(f"kpg_in{s}") for s in range(2)]
        vpg_in = [sem(f"vpg_in{b}") for b in range(NB)]
        kcT_done, kcT_evac, sc_done = sem("kcT_done"), sem("kcT_evac"), sem("sc_done")
        fs_done, smp_ok, ss_done, smax_done, sexp_done, sp_ready = (sem("fs_done"), sem("smp_ok"), sem("ss_done"),
                                                                  sem("smax_done"), sem("sexp_done"), sem("sp_ready"))
        spT_done, spT_evac, spv_done = sem("spT_done"), sem("spT_evac"), sem("spv_done")
        gh_done = sem("gh_done")
        csum_done, vsum_done, gl_done, vns_ok = sem("csum_done"), sem("vsum_done"), sem("gl_done"), sem("vns_ok")
        head_ok, gain_ok = sem("head_ok"), sem("gain_ok")
        own_done, own_T, ats_ok = sem("own_done"), sem("own_T"), sem("ats_ok")
        cm_done, cx_done, cs_done, cv_done, cr_done, cy_done, cyo_done = (sem("cm_done"), sem("cx_done"), sem("cs_done"),
                                                                       sem("cv_done"), sem("cr_done"), sem("cy_done"), sem("cyo_done"))
        ws_in, ws_Tps, ws_ok, w4_ps, w4_ok, bs_in = (sem("ws_in"), sem("ws_Tps"), sem("ws_ok"), sem("w4_ps"),
                                                    sem("w4_ok"), sem("bs_in"))
        g_done, vn_T, vn_ok, mix_done, mix_ok = sem("g_done"), sem("vn_T"), sem("vn_ok"), sem("mix_done"), sem("mix_ok")
        yT_done, y_ok, stored = sem("yT_done"), sem("y_ok"), sem("stored")
        vm_done, vx_done, vs_done, vv_done, vr_done, vy_done = (sem("vm_done"), sem("vx_done"), sem("vs_done"),
                                                             sem("vv_done"), sem("vr_done"), sem("vy_done"))
        ws_masked, gm_done, vm2_done, lfe_ok, glu_stored = sem("ws_masked"), sem("gm_done"), sem("vm2_done"), sem("lfe_ok"), sem("glu_stored")

        block = ctx.enter_context(nc.Block())

        w_in = i["w_in_ab"][0].rearrange("(k p) n -> p k n", p=P)
        w_out = i["w_out_ab"][0].rearrange("(k p) n -> p k n", p=P)
        w_inc = i["w_in_c"][0].rearrange("(k p) n -> p k n", p=P)
        w_outc = i["w_out_c"][0].rearrange("(k p) n -> p k n", p=P)

        def col(ap):
            return ap.rearrange("(k p) -> k p", p=P)

        SMALL = ((V_MIX[0], i["norm_mix_g"].rearrange("l (k p) -> (l k) p", p=P)),
                 (V_FFN[0], i["norm_ffn_g"].rearrange("l (k p) -> (l k) p", p=P)),
                 (V_CB, col(i["conv_b"][0])), (V_CG, col(i["conv_ln_g"][0])), (V_CL, col(i["conv_ln_b"][0])),
                 (V_SG, col(i["sgu_ln_g"][0])), (V_SB, col(i["sgu_ln_b"][0])))

        @block.sync
        def _(sp):
            def load(b, even, lo, hi):
                if not (isinstance(b, int) and b < 2):
                    sp.wait_ge(lo_done, 2 * b - 2)
                for dst, src in (lo, hi):
                    sp.dma_start(w_raw[:, even, dst[0]:dst[1], dst[2]:dst[3]], src).then_inc(raw_in[even], 16)

            def by_rows(w, c0):
                return [((4 * s, 4 * s + 4, 0, 256), w[:, 4 * s:4 * s + 4, c0:c0 + 256]) for s in range(2)]

            for r0, src in SMALL[1::2]:
                sp.dma_start(rows[r0:r0 + src.shape[0], :], src).then_inc(vec_in, 16)
            sp.dma_start(cw_nat[:, :], i["conv_w"][0]).then_inc(vec_in, 16)
            for g in range(4):
                c0, c1 = 256 * g, 256 * g + 256
                sp.dma_start(x_nat[0:NS, 0, c0:c1], i["x_sample"].rearrange("b q d -> (b q) d")[:, c0:c1]).then_inc(x_in[g], 16)
                sp.dma_start(x_nat[:, 1:TT, c0:c1],
                             i["x_prompt"][0].rearrange("(t p) d -> p t d", p=P)[:, :, c0:c1]).then_inc(x_in[g], 16)
                if g % 2 == 1:
                    load(g // 2, g // 2, *[((0, KT, P * s, P * s + P), w_in[:, :, DA * s + P * (g // 2):DA * s + P * (g // 2) + P])
                                 for s in range(2)])
            sp.dma_start(pt_sb[:, :], i["page_table"].rearrange("(a b) g -> a (b g)", a=1)).then_inc(pt_in, 16)
            sp.wait_ge(pt_in, 16)
            n_pool = i["cache_k"].shape[1]
            page = [sp.value_load(pt_sb[0:1, s:s + 1], min_val=0, max_val=n_pool - 1) for s in range(NB * PAGES)]
            lf_rows = i["cache_logf"][0].rearrange("n k h -> (n k) h")
            sp.wait_ge(st_T, 1)
            for b in range(NB):
                for g in range(PAGES):
                    sp.dma_start(lf_pg[:, g, b, :],
                                 lf_rows[bass.ds(page[PAGES * b + g] * PAGE, PAGE), :]).then_inc(lf_in, 16)
            for b in range(2, CT):
                load(b, b % 2, *[((0, KT, P * s, P * s + P), w_in[:, :, DA * s + P * b:DA * s + P * b + P])
                                 for s in range(2)])
            def new_history():
                sp.wait_ge(glu_nat_ok, 2)
                for b in range(NB):
                    sp.dma_start(o["conv_sample"][0, b, HIST - NQ:, :],
                                   glu_nat[NQ * b:NQ * b + NQ, 0, :]).then_inc(glu_stored, 16)
                sp.dma_start(o["conv_prompt"][0, 0], glu_nat[0:HIST, 1, :]).then_inc(glu_stored, 16)

            for m in range(6):
                if m == 4:
                    new_history()
                b = N_NAT // 2 + m
                load(b, b % 2, *by_rows(w_in, 2 * DA + 256 * m))

            def gather(cache, slot, b, arrived):
                src = cache[0].rearrange("n k h d -> (n k) (h d)")
                for g in range(PAGES):
                    sp.dma_start(slot[:, g, :], src[bass.ds(page[PAGES * b + g] * PAGE, PAGE), :]).then_inc(arrived, 16)

            def keys(b):
                if b == 0:
                    sp.wait_ge(nat_ready, 4 * TT)
                if b >= 2:
                    sp.wait_ge(kcT_done, 2 * (b - 1))
                gather(i["cache_k"], k_pg[:, b % 2], b, kpg_in[b % 2])

            for m in range(4):
                b = N_OUT // 2 + m
                if m == 3:
                    keys(0)
                    keys(1)
                    sp.wait_ge(prep_done, 1)
                    for j in range(4):
                        sp.wait_ge(s_done, QT * (2 * j + 2))
                        gather(i["cache_v"], v_pg[j], j, vpg_in[j])
                        gather(i["cache_v"], v_pg[4 + j], 4 + j, vpg_in[4 + j])
                    for b2 in range(2, NB):
                        keys(b2)
                load(b, b % 2, *by_rows(w_out, 256 * m))

            def ffn_blocks(layer):
                up = i["w_ff_up"][layer].rearrange("(k p) n -> p k n", p=P)
                down = i["w_ff_down"][layer].rearrange("(k p) n -> p k n", p=P)
                with sp.Fori(0, CHUNKS) as c:
                    for m in range(4):
                        load(N_FF[layer] // 2 + 8 * c + m, m % 2,
                             *[((4 * s, 4 * s + 4, 0, 256),
                                up[:, 4 * s:4 * s + 4, bass.ds(c * D + 256 * m, 256)]) for s in range(2)])
                    for m in range(4):
                        load(N_FF[layer] // 2 + 8 * c + 4 + m, m % 2,
                             *[((4 * s, 4 * s + 4, 0, 256),
                                down[:, bass.ds(c * KT + 4 * s, 4), 256 * m:256 * m + 256]) for s in range(2)])

            ffn_blocks(0)
            for m in range(8):
                b = N_INC // 2 + m
                load(b, b % 2, *by_rows(w_inc, (D + 256 * m) % (2 * D)))
            for m in range(4):
                b = N_OUTC // 2 + m
                load(b, b % 2, *by_rows(w_outc, 256 * m))
            ffn_blocks(1)
            for g, (c0, c1) in enumerate(((0, 512), (512, 768), (768, 1024))):
                sp.wait_ge(y_ok, c1 // P)
                sp.dma_start(o["y_prompt"][0].rearrange("(t p) d -> p t d", p=P)[:, :, c0:c1],
                             y_nat[:, 1:TT, c0:c1]).then_inc(stored, 16)
                sp.dma_start(o["y_sample"].rearrange("b q d -> (b q) d")[:, c0:c1],
                             y_nat[0:NS, 0, c0:c1]).then_inc(stored, 16)
            sp.wait_ge(stored, 6 * 16)

        @block.gpsimd
        def _(pool):
            stored_by_pool = sem("stored_by_pool")
            n_stores = [0]

            def store(dst, src):
                pool.dma_start(dst, src).then_inc(stored_by_pool, 16)
                n_stores[0] += 1

            link = Chain(pool, pool_seq)

            def mask(ap, pattern, op, base, mult, fill):
                link(pool.affine_select(out=ap, in_=ap, compare_op=op, fill=fill, base=base,
                                        pattern=pattern, channel_multiplier=mult))

            link(pool.memset(ident[:, :], 0.0))
            mask(ident[:, :], [[-1, P]], ALU.not_equal, 0, 1, 1.0)
            link(pool.memset(ones[:, :], 1.0))
            link(pool.memset(eps[:, 0:1], RMS_EPS))
            link(pool.memset(eps[:, 1:2], LN_EPS))
            link(pool.memset(wf_raw[:, :, :], 0.0))
            pool.memset(r_nat[:, :], 1.0).then_inc(consts, 1)
            for g in range(2):
                pool.dma_start(st_nat[0:4 * HIST, g, :],
                               i["state_conv"][0, 4 * g:4 * g + 4].rearrange("b w c -> (b w) c")).then_inc(st_in, 16)
            pool.dma_start(wf_raw[:, :, 0:H], w_in[:, :, 2 * DA + 3 * H * HD:]).then_inc(wfg_in, 16)
            pool.dma_start(qk_gain[:, 0, :], i["q_norm_g"][0:1, :].broadcast_to([P, HD])).then_inc(bc_in, 16)
            pool.dma_start(qk_gain[:, 1, :], i["k_norm_g"][0:1, :].broadcast_to([P, HD])).then_inc(bc_in, 16)
            pool.dma_start(bf_c[:, :], i["b_forget"].rearrange("a h -> h a")).then_inc(bc_in, 16)
            link(pool.memset(tri[:, :], 1.0))
            mask(tri[:, :], [[1, P]], ALU.is_ge, 0, -1, 0.0)
            link(pool.memset(glu_p[:, :, 0:HIST], 0.0))
            link(pool.memset(ident_b[:, :], 0.0))
            mask(ident_b[:, :], [[-1, P]], ALU.not_equal, 0, 1, 1.0)
            link(pool.memset(mask_b[:, :], 0.0))
            mask(mask_b[:, :], [[-1, P]], ALU.is_ge, 0, 1, NEG)
            link(pool.memset(maskT_b[:, :, :], 0.0))
            for g in range(2):
                m4 = maskT_b[:, g, :].rearrange("p (b h q) -> p b h q", b=4, h=H)
                mask(m4, [[-NQ, 4], [0, H], [0, NQ]], ALU.is_ge, -4 * NQ * g, 1, NEG)
                mask(m4, [[NQ, 4], [0, H], [1, NQ]], ALU.is_ge, 4 * NQ * g, -1, NEG)
            link(pool.memset(sel[:, :, :], 0.0))
            for g in range(2):
                mask(sel[:, g, :].rearrange("p (b h q) -> p b h q", b=4, h=H), [[-H, 4], [-1, H], [0, NQ]],
                     ALU.not_equal, -4 * H * g, 1, 1.0)
            link(pool.memset(heads[:, :, :], 1.0))
            mask(heads[:, :, :], [[-HQ, 4], [-NQ, H]], ALU.is_ge, 0, 1, 0.0)
            mask(heads[:, :, :], [[HQ, 4], [NQ, H]], ALU.is_ge, NQ - 1, -1, 0.0)
            link(pool.tensor_tensor(heads[:, 0:2, :], heads[:, 0:2, :], heads[:, 2:4, :], ALU.add))
            link(pool.tensor_tensor(head_is[:, :], heads[:, 0, :], heads[:, 1, :], ALU.add))
            pool.memset(f_aug[:, :, :, :], 1.0).then_inc(consts, 1)

            def square_sums():
                done = norm[0] * KT
                for k in range(1, KT):
                    pool.wait_ge(sq_done, done + k + 1)
                    if k > 1:
                        pool.wait_ge(ssq_done, norm[0] * (KT - 1) + k - 1)
                    pool.tensor_tensor(ssq[:, :], ssq[:, :], sq[:, k % 2, :], ALU.add).then_inc(ssq_done, 1)
                norm[0] += 1

            norm = [1]

            pool.wait_ge(logf_ok, 1)
            logf = f_small[:, :].rearrange("p (t h) -> p t h", h=H)
            store(o["logf_prompt"][0, 0].rearrange("(t p) h -> p t h", p=P), logf[:, 1:TT, :])
            store(o["logf_sample"][0].rearrange("b q h -> (b q) h"), logf[0:NS, 0, :])
            store(o["conv_sample"][0][:, 0:HIST - NQ, :], i["state_conv"][0][:, NQ:, :])
            link(pool.affine_select(out=lf_exp[:, :, :], in_=logf[0:NS, 0:1, :].broadcast_to([NS, NB, H]),
                                    compare_op=ALU.is_ge, fill=0.0, base=0, pattern=[[-NQ, NB], [0, H]],
                                    channel_multiplier=1))
            pool.affine_select(out=lf_exp[:, :, :], in_=lf_exp[:, :, :], compare_op=ALU.is_ge, fill=0.0,
                               base=NQ - 1, pattern=[[NQ, NB], [0, H]], channel_multiplier=-1).then_inc(lfe_ok, 1)
            for c in range(CT):
                pool.wait_ge(glu_done, c + 1)
                if c >= 2:
                    pool.wait_ge(psum_red, c - 1)
                window = glu_window(c)
                taps = conv_wT[:, c, 0:TAPS].rearrange("p (a b w) -> p a b w", a=1, b=1).broadcast_to([P, NB, NQ, TAPS])
                pool.tensor_tensor(prod[c % 2][:, :, :, :], window, taps, ALU.mult).then_inc(prod_done, 1)

            for m in range(4 * TT):
                blk, t = m // TT, m % TT
                n = NS if t == 0 else P
                buf, head = nat_buf[0:n, m % 3], n_small[0:n, 4 + m % 2, :]
                pool.wait_ge(head_ok, m + 1)
                pool.wait_ge(nat_evac, m + 1)
                if m >= 3:
                    pool.wait_ge(aug_done, m - 2)
                    if m - 3 >= 2 * TT:
                        pool.wait_ge(k_stored[m % 3], 16 * len([u for u in range(2 * TT, m - 2) if u % 3 == m % 3]))
                link(pool.tensor_tensor(buf[:, :, 0:HD], nat_raw[0:n, m % 2, :].rearrange("p (h d) -> p h d", h=4),
                                        head.rearrange("p (h a) -> p h a", a=1).broadcast_to([n, 4, HD]), ALU.mult))
                if m == 0:
                    pool.wait_ge(fc_ok, 1)
                    pool.wait_ge(gain_ok, 1)
                pool.tensor_copy(buf[:, :, HD:HD + 2],
                                 f_aug[0:n, blk // 2, H * t + 4 * (blk % 2):H * t + 4 * (blk % 2) + 4, :])
                pool.tensor_tensor(buf[:, :, 0:HD], buf[:, :, 0:HD],
                                   qk_gain[0:n, blk // 2:blk // 2 + 1, :].broadcast_to([n, 4, HD]), ALU.mult)\
                    .then_inc(nat_ready, 1)
                if m >= 2 * TT:
                    pool.wait_ge(nat_ready, m + 1)
                    h0 = 4 * (blk - 2)
                    dst = (o["k_sample"][0].rearrange("b q h d -> (b q) h d")[:, h0:h0 + 4, :] if t == 0 else
                           o["k_prompt"][0, 0, P * (t - 1):P * t, h0:h0 + 4, :])
                    pool.dma_start(dst, nat_buf[0:n, m % 3, :, 0:HD]).then_inc(k_stored[m % 3], 16)
            pool.wait_ge(nat_evac, 6 * TT)
            store(o["v_prompt"][0, 0].rearrange("(t p) h d -> p t (h d)", p=P), v_nat[:, 1:TT, :])
            store(o["v_sample"][0].rearrange("b q h d -> (b q) (h d)"), v_nat[0:NS, 0, :])

            pool.wait_ge(nat_done, 6 * TT)
            pool.memset(q_bd[:, :, :, :], 0.0).then_inc(bd_zero, 1)
            pool.wait_ge(conv_done, CT * TAPS)
            pool.wait_ge(psum_red, CT)
            link(pool.tensor_tensor(cs_f[:, CT - 1, :], c_f[:, 0, :], c_f[:, 1, :], ALU.add))
            link(pool.tensor_tensor(cs_f[:, CT - 1, :], cs_f[:, CT - 1, :], c_f[:, 2, :], ALU.add))
            pool.tensor_tensor(cs_f[:, CT - 1, :], cs_f[:, CT - 1, :], c_f[:, 3, :], ALU.add).then_inc(csum_done, 1)
            for c in range(1, CT):
                pool.wait_ge(cs_done, c + 1)
                a_ = pool.tensor_tensor(cs_f[:, 0, :], cs_f[:, 0, :], cs_f[:, c, :], ALU.add)
                if c < CT - 1:
                    link(a_)
            a_.then_inc(csum_done, 1)
            square_sums()
            pool.wait_ge(ml_done, 1)
            pool.wait_ge(tile_done, ordinal(N_OUT))
            pool.dma_start(ws_nat[:, :, :], i["w_spatial"][0].rearrange("h i j -> i h j")).then_inc(ws_in, 16)
            pool.dma_start(bs_b[:, :, :], i["b_spatial"][0:1].broadcast_to([P, H, P])).then_inc(bs_in, 16)
            link(pool.memset(rep4[:, :, :], 0.0))
            mask(rep4[:, :, :], [[0, NB], [-1, NQ]], ALU.not_equal, 0, 1, 1.0)
            link(pool.memset(blk4[:, :, :], 1.0))
            mask(blk4[:, :, :], [[-NQ, NB], [0, NQ]], ALU.is_ge, 0, 1, 0.0)
            link(pool.affine_select(out=blk4[:, :, :], in_=blk4[:, :, :], compare_op=ALU.is_ge, fill=0.0,
                                    base=NQ - 1, pattern=[[NQ, NB], [0, NQ]], channel_multiplier=-1))
            square_sums()
            pool.wait_ge(ws_Tps, 2)
            pool.wait_ge(ws_ok, 2)
            for h in range(H):
                sel_ = pool.affine_select(out=ws_T[:, h, :], in_=ws_T[:, h, :], compare_op=ALU.is_ge, fill=0.0,
                                          base=0, pattern=[[1, P]], channel_multiplier=-1)
            sel_.then_inc(ws_masked, 1)
            for index in range(2):
                for k in range(1, KT):
                    if index == 0:
                        pool.wait_ge(g_done, k + 1)
                        first = v_f[:, 0, :] if k == 1 else vq_f[:, 0, :]
                        a_ = pool.tensor_tensor(vq_f[:, 0, :], first, v_f[:, k, :], ALU.add)
                    else:
                        pool.wait_ge(vs_done, k + 1)
                        a_ = pool.tensor_tensor(vq_f[:, 0, :], vq_f[:, 0, :], vq_f[:, k, :], ALU.add)
                    if k < KT - 1:
                        link(a_)
                a_.then_inc(vsum_done, 1)
            base = 8 * CHUNKS
            for k in range(KT):
                pool.wait_ge(gh_done, k + 1)
                pool.tensor_tensor(A_lo[:, k, :], a_f[:, k % 2, :], A_hi[:, k, :].bitcast(F32), ALU.subtract)\
                    .then_inc(gl_done, 1)
            pool.wait_ge(vns_ok, KT)
            store(o["chunk_v"][0].rearrange("b q d -> (b q) d"), vn_s[:, :])
            square_sums()
            for s in range(3):
                pool.wait_ge(k_stored[s], 16 * len([m for m in range(2 * TT, 4 * TT) if m % 3 == s]))
            pool.wait_ge(stored_by_pool, n_stores[0] * 16)

        @block.tensor
        def _(pe):
            def tile(j, n, hi, lo, first_waits=None, k0=0, kn=KT):
                pe.wait_ge(lo_done, n + 1)
                pe.wait_ge(evac_done, ordinal(n) - 2)
                s = j % 2
                for k in range(KT):
                    if first_waits is not None:
                        first_waits(k)
                    for wt, mv, at_ in ((w_hi, hi, 0), (w_lo, hi, 1), (w_hi, lo, 2)):
                        for half in range(2):
                            mm = pe.matmul(ps[:, 2 * s + half, 0:HALF], wt[:, j % 4, k, :],
                                           mv[:, k, half * HALF:(half + 1) * HALF],
                                           start=(k == 0 and at_ == 0), stop=(k == KT - 1 and at_ == 2))
                mm.then_inc(tile_done, 1)

            def statistics(index):
                pe.wait_ge(ssq_done, (index + 1) * (KT - 1))
                for half in range(2):
                    mm = pe.matmul(ps[:, 6 + half, 0:HALF], ones[:, :], ssq[:, half * HALF:(half + 1) * HALF],
                                   start=True, stop=True)
                mm.then_inc(stat_done, 1)

            def turn_vectors():
                pe.wait_ge(vec_in, 8 * 16)
                pe.transpose(ps[:, 4, 0:60], rows[:, :], ident[0:60, 0:60])
                for c in range(CT):
                    mm = pe.transpose(ps[:, 5, 32 * c:32 * c + TAPS], cw_nat[:, P * c:P * c + P], ident[0:TAPS, 0:TAPS])
                mm.then_inc(vec_T, 1)

            pe.wait_ge(consts, 1)
            for k in range(KT):
                if k == 2:
                    turn_vectors()
                pe.wait_ge(x_in[k // 2], 32)
                if k >= 2:
                    pe.wait_ge(evac_done, k - 1)
                    pe.wait_ge(xc_done, k - 1)
                for t in range(TT):
                    n, (c0, c1) = (NS if t == 0 else P), tok(t)
                    bank, off = (0, c0) if t < 3 else (1, c0 - tok(3)[0])
                    mm = pe.transpose(ps[:, 2 * (k % 2) + bank, off:off + n], x_nat[0:n, t, P * k:P * k + P],
                                      ident[0:n, 0:n])
                mm.then_inc(tile_done, 1)
            pe.wait_ge(st_in, 32)
            for g in range(2):
                for c in range(CT):
                    mm = pe.transpose(ps[:, 6 + g, 120 * c:120 * c + 4 * HIST], st_nat[0:4 * HIST, g, P * c:P * c + P],
                                      ident[0:4 * HIST, 0:4 * HIST])
            mm.then_inc(st_T, 1)

            def forget_gates():
                pe.wait_ge(vec_ok, 2)
                pe.wait_ge(wfg_ok, 2)
                for k in range(KT):
                    for wt, mv, at_ in ((wf_hi, A_hi, 0), (wf_lo, A_hi, 1), (wf_hi, A_lo, 2)):
                        for half in range(2):
                            mm = pe.matmul(ps[:, 4 + half, 0:HALF], wt[:, k, :], mv[:, k, half * HALF:(half + 1) * HALF],
                                           start=(k == 0 and at_ == 0), stop=(k == KT - 1 and at_ == 2))
                mm.then_inc(fg_done, 1)

            def turn_gates():
                pe.wait_ge(logT_ok, 1)
                for t in range(TT):
                    c0, c1 = tok(t)
                    mm = pe.transpose(ps[0:c1 - c0, 4, H * t:H * t + H], gate[:, 3, c0:c1], ident[0:H, 0:H])
                mm.then_inc(log_T, 1)

            def xg_ready(index):
                return lambda k: pe.wait_ge(xl_done, KT * index + k + 1)

            pe.wait_ge(xc_done, KT)
            for j in range(8):
                tile(j, N_GLU + j, A_hi, A_lo, xg_ready(0) if j == 0 else None)
                if j == 1:
                    pe.wait_ge(vec_ok, 4)
                    statistics(0)
                    forget_gates()
                if j == 3:
                    turn_gates()
                if j == 5:
                    pe.wait_ge(logf_ok, 1)
                    pe.wait_ge(consts, 2)
                    logf = f_small[:, :]
                    pe.matmul(ps[:, 5, 0:QT * H], tri[:, :], logf[:, H:TT * H], start=True, stop=False,
                              skip_group_check=True)
                    for s in range(QT - 1):
                        for t in range(s + 1, QT):
                            mm = pe.matmul(ps[:, 5, H * t:H * t + H], ones[:, :], logf[:, H * (s + 1):H * (s + 2)],
                                           start=False, stop=(s == t - 1), skip_group_check=True)
                    mm.then_inc(fc_done, 1)

            def forget_sums():
                pe.wait_ge(lf_in, NB * PAGES * 16)
                pe.wait_ge(lfe_ok, 1)
                pe.wait_ge(glu_nat_ok, 2)
                lf0, lf1 = (lf_pg[:, g].rearrange("p b h -> p (b h)") for g in range(2))
                lfe = lf_exp[:, :, :].rearrange("p b h -> p (b h)")
                f = ps[0:NB * H, 6, :]
                pe.matmul(f[:, 0:PAGE], lf0, tri[:, :], start=True, stop=False, skip_group_check=True)
                pe.matmul(f[:, PAGE:2 * PAGE], lf1, tri[:, :], start=False, stop=False, skip_group_check=True)
                pe.matmul(f[:, PAGE:2 * PAGE], lf0, ones[:, :], start=False, stop=False, skip_group_check=True)
                pe.matmul(f[:, NEWC:KS], lfe, tri[0:NS, 0:NS], start=False, stop=False, skip_group_check=True)
                pe.matmul(f[:, NEWC:KS], lf0, ones[:, 0:NS], start=False, stop=False, skip_group_check=True)
                pe.matmul(f[:, NEWC:KS], lf1, ones[:, 0:NS], start=False, stop=True,
                          skip_group_check=True).then_inc(fs_done, 1)

            def turn_heads(m):
                t, (c0, c1) = m % TT, tok(m % TT)
                n = c1 - c0
                pe.wait_ge(nat_ready, m + 1)
                if m >= 2:
                    pe.wait_ge(aug_evac, m - 1)
                for h in range(4):
                    mm = pe.transpose(ps[0:HD + 2, 4 + m % 2, P * h:P * h + n], nat_buf[0:n, m % 3, h, :],
                                      ident[0:n, 0:n])
                mm.then_inc(aug_done, 1)

            def turn_glu():
                pe.wait_ge(glu_done, CT)
                pe.wait_ge(sqrt_done, 1)
                for c in range(CT):
                    mm = pe.transpose(ps[0:NS, 6, P * c:P * c + P], glu_new[:, c, :], ident[:, :])
                mm.then_inc(glu_nT, 1)
                for c in range(CT):
                    mm = pe.transpose(ps[0:HIST, 7, P * c:P * c + P], glu_p[:, c, S:S + HIST], ident[:, :])
                mm.then_inc(glu_nT, 1)

            pe.wait_ge(evac_done, ordinal(7))
            pe.wait_ge(fc_ok, 1)
            for m in range(6 * TT):
                blk, t = m // TT, m % TT
                if t == 0:
                    pe.wait_ge(lo_done, N_NAT + 2 * blk + 2)
                if m >= 4:
                    pe.wait_ge(nat_evac, m - 3)
                if m == 2:
                    turn_glu()
                if m == 10:
                    forget_sums()
                c0 = 0 if t == 0 else tok(t)[0]
                s = (2 * blk) % 4
                for k in range(KT):
                    for wt, mv, at_ in ((w_hi, A_hi, 0), (w_lo, A_hi, 1), (w_hi, A_lo, 2)):
                        mm = pe.matmul(ps[:, m % 4, 0:256], mv[:, k, c0:c0 + P], wt[:, s:s + 2, k, :],
                                       start=(k == 0 and at_ == 0), stop=(k == KT - 1 and at_ == 2))
                mm.then_inc(nat_done, 1)
                if 2 <= m < 4 * TT + 2:
                    turn_heads(m - 2)

            def scores(s):
                h, q = s // QT, s % QT
                if s == 0:
                    pe.wait_ge(nat_evac, 6 * TT)
                    pe.wait_ge(aug_evac, 4 * TT)
                if s >= 3:
                    pe.wait_ge(exp_done, s - 2)
                n = P * (q + 1)
                pe.matmul(ps[:, s % 3, 0:n], qT[0:HD + 2, h, NS + P * q:NS + P * q + P], kT[0:HD + 2, h, NS:NS + n],
                          start=True, stop=False, skip_group_check=True)
                pe.matmul(ps[:, s % 3, P * q:n], ident_b[:, :], mask_b[:, :], start=False, stop=True,
                          skip_group_check=True).then_inc(s_done, 1)

            def turn_probs(s):
                pe.wait_ge(p_ready, s + 1)
                if s >= 2:
                    pe.wait_ge(pT_evac, s - 1)
                for j in range(s % QT + 1):
                    mm = pe.transpose(ps[:, 3 + s % 2, P * j:P * j + P], prob[:, s % 2, P * j:P * j + P], ident[:, :])
                mm.then_inc(pT_done, 1)

            def values(h):
                pe.wait_ge(pT_evac, QT * (h + 1))
                if h >= 2 and h % 2 == 0:
                    pe.wait_ge(ml_done, h // 2)
                half = HD * (h % 2)
                for j in range(QT):
                    mm = pe.matmul(ps[half:half + HD, 5, P * j:S],
                                   v_nat[:, 1 + j, HD * h:HD * h + HD],
                                   pT[h % 2][:, S * j:S * j + S - P * j],
                                   start=(j == 0), stop=(j == QT - 1), skip_group_check=True)
                mm.then_inc(pv_done, 1)

            def column_sums(src, ready, count, done):
                pe.wait_ge(ready, count)
                for half in range(2):
                    mm = pe.matmul(ps[:, 6 + half, 0:HALF], ones[:, :], src[:, half * HALF:(half + 1) * HALF],
                                   start=True, stop=True)
                mm.then_inc(done, 1)

            n_items = H * QT
            scores(0)
            scores(1)
            for s in range(n_items):
                if s + 2 < n_items:
                    scores(s + 2)
                turn_probs(s)
                if s % QT == 1 and s > QT:
                    values(s // QT - 1)
                if s == LN_MEAN:
                    pe.wait_ge(smp_ok, 1)
                    column_sums(cs_f[:, CT - 1, :], csum_done, 1, cm_done)
                if s == LN_VAR:
                    pe.wait_ge(cx_done, CT)
                    column_sums(cs_f[:, 0, :], csum_done, 2, cv_done)
            values(H - 1)

            def turn_pages(b):
                pe.wait_ge(kpg_in[b % 2], 32 * (b // 2 + 1))
                for g in range(PAGES):
                    u = 2 * b + g
                    if u >= 2:
                        pe.wait_ge(kcT_evac, u - 1)
                    else:
                        pe.wait_ge(pT_evac, H * QT)
                    for p2 in range(PAIRS):
                        mm = pe.transpose(ps[:, 3 + g, P * p2:P * p2 + P], k_pg[:, b % 2, g, P * p2:P * p2 + P],
                                          ident[:, :])
                    mm.then_inc(kcT_done, 1)

            def sample_scores(b):
                g, b4 = b // 4, b % 4
                out = ps[:, g, :]
                if b4 == 0:
                    if g == 0:
                        pe.wait_ge(exp_done, H * QT)
                        pe.wait_ge(smp_ok, 1)
                        pe.wait_ge(prep_done, 1)
                    ones_row = ones[0:NB * H, :]
                    pe.matmul(out[:, 0:KS], sel[:, g, :], nf_T[:, :], start=True, stop=False, skip_group_check=True)
                    for c0, c1 in ((0, 128), (128, 256), (256, KS)):
                        pe.matmul(out[:, c0:c1], self_q[:, g, :], ones_row[:, 0:c1 - c0], start=False, stop=False,
                                  skip_group_check=True)
                    pe.matmul(out[:, NEWC:KS], maskT_b[:, g, :], ident_b[0:NS, 0:NS], start=False, stop=False,
                              skip_group_check=True)
                    for p2 in range(PAIRS):
                        pe.matmul(out[:, NEWC:KS], q_bd[:, p2, 4 * g:4 * g + 4, :].rearrange("p b c -> p (b c)"), kn_T[:, p2, :],
                                  start=False, stop=False, skip_group_check=True)
                pe.wait_ge(kcT_evac, 2 * (b + 1))
                for p2 in range(PAIRS):
                    mm = pe.matmul(out[HQ * b4:HQ * b4 + HQ, 0:NEWC], q_bd[:, p2, b, :], kc_T[b % 2][:, p2, :],
                                   start=False, stop=(p2 == PAIRS - 1), skip_group_check=True)
                mm.then_inc(sc_done, 1)

            def turn_sample(g):
                pe.wait_ge(sp_ready, g + 1)
                out = ps[:, 2, :]
                if g == 1:
                    pe.wait_ge(spT_evac, 1)
                pe.transpose(out[:, 0:P], prob_s[:, g, 0:P], ident[:, :])
                pe.transpose(out[:, P:2 * P], prob_s[:, g, P:2 * P], ident[:, :])
                pe.transpose(out[0:NS, 2 * P:3 * P], prob_s[:, g, NEWC:KS], ident[:, :]).then_inc(spT_done, 1)

            def sample_new_values(g):
                pe.wait_ge(spT_evac, g + 1)
                if g == 0:
                    pe.wait_ge(ml_done, PAIRS)
                else:
                    pe.wait_ge(cr_done, 1)
                pe.matmul(ps[:, 5 + g, :], p_sT[0:NS, g, 2, :], v_nat[0:NS, 0, :], start=True, stop=False,
                          skip_group_check=True)

            def sample_values(b):
                g, c = b // 4, HQ * (b % 4)
                pe.wait_ge(vpg_in[b], 32)
                for u in range(PAGES):
                    mm = pe.matmul(ps[c:c + HQ, 5 + g, :], p_sT[:, g, u, c:c + HQ], v_pg[b][:, u, :], start=False,
                                   stop=(u == PAGES - 1), skip_group_check=True)
                mm.then_inc(spv_done, 1)

            def turn_values(g):
                pe.wait_ge(own_done, g + 1)
                for p2 in range(PAIRS):
                    mm = pe.transpose(ps[:, 3 + g, P * p2:P * p2 + P], own[:, g, P * p2:P * p2 + P], ident[:, :])
                mm.then_inc(own_T, 1)

            turn_pages(0)
            for b in range(NB):
                if b + 1 < NB:
                    turn_pages(b + 1)
                sample_scores(b)
                if b == 6:
                    turn_sample(0)
            sample_new_values(0)
            for b in range(4):
                sample_values(b)
            turn_sample(1)
            sample_new_values(1)
            for b in range(4, NB):
                sample_values(b)
                if b == 4:
                    turn_values(0)
            turn_values(1)

            def merged_ready(k):
                if k < CT:
                    pe.wait_ge(cyo_done, k + 1)
                else:
                    pe.wait_ge(ml_done, PAIRS + 2)

            pe.wait_ge(spT_evac, 2)
            for j in range(8):
                tile(j, N_OUT + j, A_hi, A_lo, merged_ready if j == 0 else None)

            def turn_y(k):
                pe.wait_ge(evac_done, ordinal(N_END - 8 + k))
                if k == 0:
                    pe.wait_ge(sqrt_done, 4)
                if k >= 2:
                    pe.wait_ge(y_ok, k - 1)
                for t in range(1, TT):
                    pe.transpose(ps[:, 4 + k % 2, P * (t - 1):P * t], xT[:, k, tok(t)[0]:tok(t)[1]], ident[:, :])
                pe.transpose(ps[0:NS, 6 + k % 2, 0:P], xT[:, k, 0:NS], ident[:, :]).then_inc(yT_done, 1)

            def ffn_chunk(layer, c, before_up=None, after_first=None, last=False):
                n0 = N_FF[layer] + 16 * c
                for j in range(8):
                    tile(j, n0 + j, B_hi, B_lo, before_up if j == 0 else None)
                    if j == 0 and after_first is not None:
                        after_first()
                base = FFA[layer] + 8 * c
                for j in range(8):
                    tile(j, n0 + 8 + j, A_hi, A_lo,
                         (lambda k: pe.wait_ge(al_done, base + k + 1)) if j == 0 else None)
                    if last and layer == 1 and j >= 1:
                        turn_y(j - 1)
                if last and layer == 1:
                    turn_y(KT - 1)

            def ffn(layer, index):
                ffn_chunk(layer, 0, xg_ready(index), lambda: statistics(index))
                with pe.Fori(1, CHUNKS - 1) as c:
                    ffn_chunk(layer, c)
                ffn_chunk(layer, CHUNKS - 1, last=True)

            FFA = [0, 8 * CHUNKS]
            ffn(0, 1)

            pe.wait_ge(ws_in, 16)
            pe.wait_ge(consts, 2)
            for h in range(H):
                mm = pe.transpose(ps[:, 4 + h // 4, P * (h % 4):P * (h % 4) + P], ws_nat[:, h, :], ident[:, :])
                if h % 4 == 3:
                    mm.then_inc(ws_Tps, 1)

            for j in range(8):
                tile(j, N_INC + j, B_hi, B_lo, xg_ready(2) if j == 0 else None)
                if j == 0:
                    statistics(2)
                if j == 2:
                    pe.wait_ge(ws_masked, 1)
                    pe.matmul(ps[0:NS, 4, 0:H * NQ], rep4[:, :, :].rearrange("p b j -> p (b j)"),
                              ws_T[0:NQ, :, 0:NQ], start=True, stop=True).then_inc(w4_ps, 1)
            for j in range(8):
                tile(j, N_INC + 8 + j, B_hi, B_lo)
                if j == 0:
                    pe.wait_ge(sqrt_done, 3)
                    column_sums(vq_f[:, 0, :], vsum_done, 1, vm_done)
                if j == SGU_VAR:
                    pe.wait_ge(vx_done, KT)
                    column_sums(vq_f[:, 0, :], vsum_done, 2, vv_done)

            for k in range(KT):
                pe.wait_ge(vy_done, k + 1)
                if k == 0:
                    pe.wait_ge(w4_ok, 1)
                if k >= 2:
                    pe.wait_ge(vn_ok, k - 1)
                    pe.wait_ge(vns_ok, k - 1)
                for c in range(QT):
                    mm = pe.transpose(ps[:, 4 + k % 2, P * c:P * c + P], v_f[:, k, NS + P * c:NS + P * c + P], ident[:, :])
                mm.then_inc(vn_T, 1)
                if k == 0:
                    pe.wait_ge(vr_done, 1)
                mm = pe.transpose(ps[0:NS, 6 + k % 2, 0:P], v_f[:, k, 0:NS], ident[:, :])
                mm.then_inc(vn_T, 1)
            for h in range(H):
                if h == 0:
                    pe.wait_ge(vn_ok, KT)
                    pe.wait_ge(vns_ok, KT)
                if h >= 2:
                    pe.wait_ge(mix_ok, h - 1)
                for c in range(QT):
                    pe.matmul(ps[:, 4 + h % 2, P * c:P * c + P], vn_p[:, c, P * h:P * h + P], ws_T[:, h, :],
                              start=True, stop=True)
                pe.matmul(ps[:, 6 + h % 2, 0:NS], vn_s[:, P * h:P * h + P], ws4[:, h].rearrange("p b q -> p (b q)"),
                          start=True, stop=True).then_inc(mix_done, 1)
            base = 8 * CHUNKS
            for j in range(8):
                tile(j, N_OUTC + j, A_hi, A_lo, (lambda k: pe.wait_ge(gl_done, k + 1)) if j == 0 else None)
            ffn(1, 3)

        @block.scalar
        def _(act):
            link = Chain(act, act_seq)

            def split_hi(j, n, wait=None):
                b = j // 2
                act.wait_ge(raw_in[b % 2], 32 * (n // 4 + 1) if isinstance(n, int) else wait)
                act.activation(w_hi[:, j % 4], w_raw[:, b % 2, :, P * (j % 2):P * (j % 2) + P], ACT.Copy)\
                   .then_inc(hi_done, 1)

            def x_hi(k, gain, hi):
                act.activation(hi[:, k, :], xT[:, k, :], ACT.Copy, scale=vec[:, gain + k:gain + k + 1]).then_inc(xh_done, 1)

            def x_square(k, index):
                if k >= 3:
                    act.wait_ge(ssq_done, index * (KT - 1) + k - 2)
                dst = ssq[:, :] if k == 0 else sq[:, k % 2, :]
                act.activation(dst, xT[:, k, :], ACT.Square).then_inc(sq_done, 1)

            def round_x(k, gain, index, hi):
                x_hi(k, gain, hi)
                x_square(k, index)

            def root(index):
                act.wait_ge(stat_done, index + 1)
                act.activation(two(r_all[:, :]), ps[:, 6:8, 0:HALF], ACT.Sqrt, bias=eps[:, 0:1], scale=1.0 / D)\
                   .then_inc(sqrt_done, 1)

            for r0, src in SMALL[0::2]:
                act.dma_start(rows[r0:r0 + src.shape[0], :], src).then_inc(vec_in, 16)

            c3 = tok(3)[0]
            for k in range(KT):
                act.wait_ge(tile_done, k + 1)
                act.activation(xT[:, k, c3:T], ps[:, 2 * (k % 2) + 1, 0:T - c3], ACT.Copy).then_inc(xc_done, 1)
                act.wait_ge(evac_done, k + 1)
                act.wait_ge(xc_done, k + 1)
                act.wait_ge(vec_ok, 1)
                x_hi(k, V_MIX[0], A_hi)
                if k == 4:
                    split_hi(0, 0)
            split_hi(1, 1)
            for k in range(KT):
                x_square(k, 0)
            act.wait_ge(wfg_in, 16)
            act.activation(wf_hi[:, :, :], wf_raw[:, :, :], ACT.Copy).then_inc(wfg_ok, 1)
            split_hi(2, 2)
            act.wait_ge(consts, 1)
            for t in range(TT):
                n = NS if t == 0 else P
                link(act.activation(x_nat[0:n, t, :], x_nat[0:n, t, :], ACT.Square, accum_out=r_nat[0:n, t:t + 1]))
            root(0)
            split_hi(3, 3)
            act.activation(r_nat[:, :], r_nat[:, :], ACT.Sqrt, bias=eps[:, 0:1], scale=1.0 / D).then_inc(rn_sqrt, 1)

            for j in range(8):
                n = N_GLU + j
                act.wait_ge(evac_done, ordinal(n))
                if j % 2 == 1:
                    if j >= 3:
                        act.wait_ge(glu_done, j // 2)
                    act.activation(a_f[:, 0, :], t_f[:, 1, :], ACT.Sigmoid).then_inc(sig_done, 1)
                split_hi(j, n + 4)
                if j == 1:
                    act.wait_ge(z_ok, 1)
                    link(act.activation(gate[:, 1, :], gate[:, 0, :], ACT.Abs, bias=bf_c[:, :]))
                    link(act.activation(gate[:, 1, :], gate[:, 1, :], ACT.Exp, scale=-1.0))
                    act.activation(gate[:, 2, :], gate[:, 1, :], ACT.Ln, bias=1.0).then_inc(ln_ok, 1)

            def nat_step(m):
                blk, t = m // TT, m % TT
                n = NS if t == 0 else P
                act.wait_ge(nat_done, m + 1)
                src = ps[0:n, m % 4, 0:256]
                if blk < 4:
                    if m >= 2:
                        act.wait_ge(nat_ready, m - 1)
                    act.activation(nat_sq[0:n, m % 2, :], src, ACT.Square, scale=r_nat[0:n, t:t + 1]).then_inc(nat_sq_done, 1)
                    act.activation(nat_raw[0:n, m % 2, :], src, ACT.Copy, scale=r_nat[0:n, t:t + 1]).then_inc(nat_evac, 1)
                else:
                    act.activation(v_nat[0:n, t, 256 * (blk - 4):256 * (blk - 3)], src, ACT.Copy,
                                   scale=r_nat[0:n, t:t + 1]).then_inc(nat_evac, 1)

            def nat_root(m):
                n = NS if m % TT == 0 else P
                act.wait_ge(nat_rs, m + 1)
                act.activation(n_small[0:n, 2 + m % 2, :], n_small[0:n, m % 2, :], ACT.Sqrt, bias=eps[0:n, 0:1],
                               scale=1.0 / HD).then_inc(nat_sqrt, 1)

            def aug_copy(m):
                t, (c0, c1) = m % TT, tok(m % TT)
                dst, h0 = (qT if m // TT < 2 else kT), 4 * (m // TT % 2)
                act.wait_ge(aug_done, m + 1)
                act.activation(dst[0:HD + 2, h0:h0 + 4, c0:c1],
                               ps[0:HD + 2, 4 + m % 2, :].rearrange("p (h c) -> p h c", h=4)[:, :, 0:c1 - c0],
                               ACT.Copy).then_inc(aug_evac, 1)

            act.wait_ge(glu_done, CT)
            for m in range(6 * TT):
                nat_step(m)
                if m < 4 * TT:
                    nat_root(m)
                if 3 <= m < 4 * TT + 3:
                    aug_copy(m - 3)
                if m == 5:
                    act.wait_ge(glu_nT, 2)
                    act.activation(glu_nat[0:NS, 0, :], ps[0:NS, 6, :], ACT.Copy).then_inc(glu_nat_ok, 1)
                    act.activation(glu_nat[0:HIST, 1, :], ps[0:HIST, 7, :], ACT.Copy).then_inc(glu_nat_ok, 1)
                if m >= TT and m % TT in (0, 2):
                    n = N_NAT + 2 * (m // TT - 1) + m % TT // 2
                    split_hi(n % 4, n + 4)
            for n in range(N_OUT - 2, N_OUT):
                split_hi(n % 4, n + 4)

            mx, rs = soft[:, 0, :], soft[:, 1, :]

            def exponent(s):
                n = P * (s % QT + 1)
                act.wait_ge(max_done, s + 1)
                if s >= 2:
                    act.wait_ge(pT_done, s - 1)
                act.activation(prob[:, s % 2, 0:n], ps[:, s % 3, 0:n], ACT.Exp, bias=mx[:, s % 4:s % 4 + 1],
                               accum_out=rs[:, s % 4:s % 4 + 1]).then_inc(exp_done, 1)

            def copy_probs(s):
                h, q = s // QT, s % QT
                act.wait_ge(pT_done, s + 1)
                if q == 0 and h == 1:
                    act.wait_ge(psum_red, CT)
                if q == 0 and h >= 2:
                    act.wait_ge(pv_done, h - 1)
                dst = pT[h % 2][:, :].rearrange("p (j c) -> p j c", c=P)
                for_j = dst[:, q:q + 3 * q + 1:3, :] if q else dst[:, 0:1, :]
                act.activation(for_j, ps[:, 3 + s % 2, 0:P * (q + 1)].rearrange("p (j c) -> p j c", c=P), ACT.Copy)\
                   .then_inc(pT_evac, 1)

            def pair_hi(p2):
                act.wait_ge(pv_done, 2 * p2 + 2)
                act.activation(A_hi[:, CT + p2, NS:T], ps[:, 5, :], ACT.Copy).then_inc(mh_done, 1)

            def sample_prep(h):
                rows_ = slice(HD * (h % 2), HD * (h % 2) + HD)
                act.activation(q_bd[rows_, h // 2, :, NQ * h:NQ * h + NQ],
                               qT[0:HD, h, 0:NS].rearrange("p (b q) -> p b q", b=NB), ACT.Copy)
                kn = act.activation(kn_T[rows_, h // 2, :], kT[0:HD, h, 0:NS], ACT.Copy)
                if h == H - 1:
                    kn.then_inc(prep_done, 1)

            def conv_square(c):
                act.wait_ge(cx_done, c + 1)
                act.activation(cs_f[:, c, :], c_f[:, c, :], ACT.Square).then_inc(cs_done, 1)

            for s in range(H * QT):
                exponent(s)
                if s == 1:
                    act.wait_ge(glu_stored, 16 * (NB + 1))
                if s >= 1:
                    copy_probs(s - 1)
                if s % (2 * QT) == 2 and s > 2 * QT:
                    pair_hi(s // (2 * QT) - 1)
                if 2 <= s < 6:
                    if s == 2:
                        act.wait_ge(bd_zero, 1)
                    sample_prep(2 * s - 4)
                    sample_prep(2 * s - 3)
                if s in (LN_MEAN + 3, LN_MEAN + 4):
                    conv_square(2 * (s - LN_MEAN - 3))
                    conv_square(2 * (s - LN_MEAN - 3) + 1)
            act.wait_ge(cv_done, 1)
            act.activation(two(r_all[:, :]), ps[:, 6:8, 0:HALF], ACT.Sqrt, bias=eps[:, 1:2], scale=1.0 / DA)\
               .then_inc(cr_done, 1)
            copy_probs(H * QT - 1)
            pair_hi(PAIRS - 1)

            def page_copy(b, g):
                act.wait_ge(kcT_done, 2 * b + g + 1)
                if b >= 2:
                    act.wait_ge(sc_done, b - 1)
                act.activation(kc_T[b % 2][:, :, P * g:P * g + P],
                               ps[:, 3 + g, :].rearrange("p (a c) -> p a c", a=PAIRS), ACT.Copy).then_inc(kcT_evac, 1)

            def sample_exp(g):
                act.wait_ge(smax_done, g + 1)
                act.activation(prob_s[:, g, :], ps[:, g, 0:KS], ACT.Exp, bias=mx[:, g:g + 1],
                               accum_out=rs[:, g:g + 1]).then_inc(sexp_done, 1)

            def sample_copy(g):
                act.wait_ge(spT_done, g + 1)
                act.activation(p_sT[:, g, 0:2, :], ps[:, 2, 0:2 * P].rearrange("p (a c) -> p a c", a=2), ACT.Copy)
                act.activation(p_sT[0:NS, g, 2, :], ps[0:NS, 2, 2 * P:3 * P], ACT.Copy).then_inc(spT_evac, 1)

            act.wait_ge(conv_done, CT * TAPS)
            act.wait_ge(glu_nT, 2)
            for b in range(NB):
                page_copy(b, 0)
                page_copy(b, 1)
                if b in (3, 4):
                    for c in (2 * (b - 3), 2 * (b - 3) + 1):
                        act.wait_ge(cy_done, c + 1)
                        act.activation(c_f[:, c, :], c_f[:, c, :], ACT.Silu, bias=vec[:, V_CL + c:V_CL + c + 1],
                                       scale=vec[:, V_CG + c:V_CG + c + 1]).then_inc(silu_done, 1)
                if b == 5:
                    sample_exp(0)
            for s in range(3):
                act.wait_ge(k_stored[s], 16 * len([m for m in range(2 * TT, 4 * TT) if m % 3 == s]))
            sample_copy(0)
            sample_exp(1)
            act.wait_ge(sc_done, NB)
            for c in range(CT):
                act.wait_ge(silu_done, c + 1)
                act.activation(A_hi[:, c, :], c_f[:, c, :], ACT.Copy).then_inc(cyh_done, 1)
            sample_copy(1)
            for g in range(2):
                act.wait_ge(ats_ok, g + 1)
                act.activation(A_hi[:, CT:KT, 16 * g:16 * g + 16], at_s[:, :, 16 * g:16 * g + 16], ACT.Copy).then_inc(mh_done, 1)

            for j in range(8):
                n = N_OUT + j
                act.wait_ge(evac_done, ordinal(n))
                round_x(j, V_FFN[0], 1, B_hi)
                split_hi(j, n + 4)

            def ffn_chunk(layer, c, last, after_first=None):
                n0, base = N_FF[layer] + 16 * c, FFA[layer] + 8 * c
                for j in range(16):
                    n = n0 + j
                    if j == 0 and after_first is not None:
                        after_first()
                    act.wait_ge(evac_done, ordinal(n))
                    if j < 8:
                        if not (isinstance(base, int) and base + j < 2):
                            act.wait_ge(al_done, base + j - 1)
                        act.activation(a_f[:, j % 2, :], t_f[:, j % 2, :], ACT.Square)
                        act.activation(A_hi[:, j, :], t_f[:, j % 2, :], ACT.Square).then_inc(ah_done, 1)
                    elif last and layer == 0:
                        round_x(j - 8, V_MIX[1], 2, B_hi)
                    if not (isinstance(n, int) and n + 4 >= N_END):
                        split_hi(j, n + 4, 32 * ((N_FF[layer] + 4) // 4 + 4 * c + j // 4 + 1) if not isinstance(n, int) else None)
                    if last and layer == 1 and j >= 8 + 1:
                        y_copy(j - 9)

            def y_copy(k):
                act.wait_ge(yT_done, k + 1)
                act.activation(y_nat[:, 1:TT, P * k:P * k + P],
                               ps[:, 4 + k % 2, :].rearrange("p (t c) -> p t c", c=P), ACT.Copy)
                act.activation(y_nat[0:NS, 0, P * k:P * k + P], ps[0:NS, 6 + k % 2, 0:P], ACT.Copy).then_inc(y_ok, 1)

            def ffn(layer, index):
                ffn_chunk(layer, 0, False, lambda: root(index))
                with act.Fori(1, CHUNKS - 1) as c:
                    ffn_chunk(layer, c, False)
                ffn_chunk(layer, CHUNKS - 1, True)

            FFA = [0, 8 * CHUNKS]
            ffn(0, 1)

            def v_square(k):
                act.wait_ge(vx_done, k + 1)
                act.activation(vq_f[:, k, :], v_f[:, k, :], ACT.Square).then_inc(vs_done, 1)

            for j in range(16):
                n = N_INC + j
                if j == 0:
                    root(2)
                act.wait_ge(evac_done, ordinal(n))
                dst = v_f[:, j, :] if j < 8 else u_f[:, j - 8, :]
                act.activation(dst, t_f[:, j % 2, :], ACT.Gelu_apprx_tanh).then_inc(g_done, 1)
                if j == 0:
                    for half in range(2):
                        act.wait_ge(ws_Tps, half + 1)
                        act.activation(ws_T[:, 4 * half:4 * half + 4, :],
                                       ps[:, 4 + half, :].rearrange("p (h c) -> p h c", h=4), ACT.Copy).then_inc(ws_ok, 1)
                split_hi(j, n + 4)
                if j in (9, 10):
                    for k in range(4 * (j - 9), 4 * (j - 8)):
                        v_square(k)
                if j == 9 + SGU_VAR:
                    act.wait_ge(vv_done, 1)
                    act.activation(two(ssq[:, :]), ps[:, 6:8, 0:HALF], ACT.Sqrt, bias=eps[:, 1:2], scale=1.0 / D)\
                       .then_inc(vr_done, 1)
                if j >= 10 + SGU_VAR and 3 * (j - 10 - SGU_VAR) < KT:
                    for k in range(3 * (j - 10 - SGU_VAR), min(KT, 3 * (j - 9 - SGU_VAR))):
                        act.wait_ge(vm2_done, k + 1)
                        act.activation(v_f[:, k, :], v_f[:, k, :], ACT.Identity, bias=vec[:, V_SB + k:V_SB + k + 1],
                                       scale=vec[:, V_SG + k:V_SG + k + 1]).then_inc(vy_done, 1)
            for k in range(KT):
                act.wait_ge(vn_T, 2 * k + 1)
                act.activation(vn_p[:, :, P * k:P * k + P], ps[:, 4 + k % 2, :].rearrange("p (c f) -> p c f", c=QT),
                               ACT.Copy).then_inc(vn_ok, 1)
            base = 8 * CHUNKS
            for k in range(KT):
                act.wait_ge(gm_done, k + 1)
                act.activation(A_hi[:, k, :], a_f[:, k % 2, :], ACT.Copy).then_inc(gh_done, 1)
            for j in range(8):
                n = N_OUTC + j
                act.wait_ge(evac_done, ordinal(n))
                round_x(j, V_FFN[1], 3, B_hi)
                split_hi(j, n + 4)
            ffn(1, 3)
            y_copy(KT - 1)

        @block.vector
        def _(dve):
            link = Chain(dve, dve_seq)

            def evacuate_to(dst, s, r=True):
                return dve.tensor_tensor(two(dst), result(s), two(r_all[:, :]), ALU.mult)

            def split_lo(j, n):
                dve.wait_ge(hi_done, n + 1)
                dve.tensor_tensor(w_lo[:, j % 4, :, :], w_raw[:, (j // 2) % 2, :, P * (j % 2):P * (j % 2) + P],
                                  w_hi[:, j % 4, :, :].bitcast(F32), ALU.subtract).then_inc(lo_done, 1)

            def rest_x(k, gain, index, hi, lo):
                dve.wait_ge(xh_done, KT * index + k + 1)
                dve.scalar_tensor_tensor(out=lo[:, k, :], in0=xT[:, k, :], scalar=vec[:, gain + k:gain + k + 1],
                                         in1=hi[:, k, :].bitcast(F32), op0=ALU.mult, op1=ALU.subtract)\
                   .then_inc(xl_done, 1)

            def invert_r(index):
                dve.wait_ge(sqrt_done, index + 1)
                link(dve.reciprocal(r_all[:, :], r_all[:, :]))

            def columns():
                dve.wait_ge(vec_T, 1)
                dve.tensor_copy(vec[:, :], ps[:, 4, 0:60]).then_inc(vec_ok, 1)
                dve.tensor_copy(conv_wT[:, :, 0:TAPS],
                                ps[:, 5, 0:32 * CT].rearrange("p (c w) -> p c w", w=32)[:, :, 0:TAPS]).then_inc(vec_ok, 1)
                dve.wait_ge(vec_ok, 1)

            c3 = tok(3)[0]
            for k in range(KT):
                dve.wait_ge(tile_done, k + 1)
                dve.tensor_copy(xT[:, k, 0:c3], ps[:, 2 * (k % 2), 0:c3]).then_inc(evac_done, 1)
                if k == 1:
                    columns()
                if k >= 1:
                    rest_x(k - 1, V_MIX[0], 0, A_hi, A_lo)
                if k == 6:
                    split_lo(0, 0)
            rest_x(KT - 1, V_MIX[0], 0, A_hi, A_lo)
            split_lo(1, 1)
            for k in range(1, KT):
                dve.wait_ge(sq_done, k + 1)
                if k > 1:
                    dve.wait_ge(ssq_done, k - 1)
                dve.tensor_tensor(ssq[:, :], ssq[:, :], sq[:, k % 2, :], ALU.add).then_inc(ssq_done, 1)
            dve.wait_ge(wfg_ok, 1)
            dve.tensor_tensor(wf_lo[:, :, :], wf_raw[:, :, :], wf_hi[:, :, :].bitcast(F32), ALU.subtract).then_inc(wfg_ok, 1)
            split_lo(2, 2)
            dve.wait_ge(bc_in, 48)
            dve.tensor_scalar(qk_gain[:, 0, :], qk_gain[:, 0, :], float(HD) ** -0.5, None, ALU.mult).then_inc(gain_ok, 1)
            dve.wait_ge(st_T, 1)
            for g in range(2):
                for c in range(CT):
                    cp = dve.tensor_copy(glu_s[:, c, 4 * g:4 * g + 4, 0:HIST],
                                         ps[:, 6 + g, 120 * c:120 * c + 4 * HIST].rearrange("p (b w) -> p b w", b=4))
                cp.then_inc(vec_ok, 1)

            def gates():
                dve.wait_ge(fg_done, 1)
                dve.tensor_tensor(two(gate[:, 0, :]), ps[0:H, 4:6, 0:HALF], two(r_all[0:H, :]), ALU.mult).then_inc(z_ok, 1)

            def log_forget():
                dve.wait_ge(z_ok, 1)
                link(dve.tensor_scalar(gate[:, 3, :], gate[:, 0, :], bf_c[:, :], 0.0, ALU.add, ALU.min))
                dve.wait_ge(ln_ok, 1)
                dve.tensor_tensor(gate[:, 3, :], gate[:, 3, :], gate[:, 2, :], ALU.subtract).then_inc(logT_ok, 1)

            def conv(steps):
                for u in range(next_step[0], min(next_step[0] + steps, CT * TAPS)):
                    pair, tap, c = u // (2 * TAPS), u % (2 * TAPS) // 2, 2 * (u // (2 * TAPS)) + u % 2
                    if tap == 0:
                        dve.wait_ge(glu_done, c + 1)
                        dve.wait_ge(consts, 2)
                        dve.tensor_scalar(c_f[:, c, NS:T], glu_p[:, c, 0:S], conv_wT[:, c, 0:1],
                                          vec[:, V_CB + c:V_CB + c + 1], ALU.mult, ALU.add).then_inc(conv_done, 1)
                    else:
                        dve.wait_ge(conv_done, u - 1)
                        dve.scalar_tensor_tensor(out=c_f[:, c, NS:T], in0=glu_p[:, c, tap:tap + S],
                                                 scalar=conv_wT[:, c, tap:tap + 1], in1=c_f[:, c, NS:T],
                                                 op0=ALU.mult, op1=ALU.add).then_inc(conv_done, 1)
                next_step[0] += steps

            def sum_taps(c):
                dve.wait_ge(prod_done, c + 1)
                link(dve.tensor_reduce(c_f[:, c, 0:NS], prod[c % 2][:, :, :, :].rearrange("p b q w -> p (b q) w"),
                                       AX_X, ALU.add))
                dve.tensor_scalar(c_f[:, c, 0:NS], c_f[:, c, 0:NS], vec[:, V_CB + c:V_CB + c + 1], None, ALU.add)\
                   .then_inc(psum_red, 1)

            next_step = [0]

            for j in range(8):
                n = N_GLU + j
                if j == 0:
                    invert_r(0)
                dve.wait_ge(tile_done, ordinal(n))
                if j >= 2:
                    dve.wait_ge(glu_done, j // 2)
                evacuate_to(t_f[:, j % 2, :], j % 2).then_inc(evac_done, 1)
                split_lo(j + 3, n + 3)
                if j == 1:
                    gates()
                if j == 2:
                    log_forget()
                if j == 3:
                    dve.wait_ge(rn_sqrt, 1)
                    link(dve.reciprocal(r_nat[:, :], r_nat[:, :]))
                if j == 4:
                    dve.wait_ge(log_T, 1)
                    dve.tensor_copy(f_small[:, :], ps[:, 4, 0:TT * H]).then_inc(logf_ok, 1)
                if j % 2 == 1:
                    c = j // 2
                    dve.wait_ge(sig_done, c + 1)
                    dve.tensor_tensor(glu_p[:, c, HIST:HIST + S], t_f[:, 0, NS:T], a_f[:, 0, NS:T], ALU.mult)
                    dve.tensor_tensor(glu_s[:, c, :, HIST:HIST + NQ],
                                      t_f[:, 0, 0:NS].rearrange("p (b q) -> p b q", b=NB),
                                      a_f[:, 0, 0:NS].rearrange("p (b q) -> p b q", b=NB), ALU.mult)
                    dve.tensor_tensor(glu_new[:, c, :], t_f[:, 0, 0:NS], a_f[:, 0, 0:NS], ALU.mult).then_inc(glu_done, 1)
                if 4 <= j:
                    if j < 7:
                        conv(CONV_GLU)
                    if j % 2 == 0:
                        sum_taps(j // 2 - 2)
                if j == 6:
                    dve.wait_ge(fc_done, 1)
                    dve.wait_ge(consts, 2)
                    dve.tensor_copy(f_aug[:, 0, H:TT * H, 0], ps[:, 5, 0:QT * H])
                    dve.tensor_scalar(f_aug[:, 1, H:TT * H, 1], ps[:, 5, 0:QT * H], -1.0, None, ALU.mult)\
                       .then_inc(fc_ok, 1)

            def sums(m):
                n = NS if m % TT == 0 else P
                dve.wait_ge(nat_sq_done, m + 1)
                dve.tensor_reduce(n_small[0:n, m % 2, :], nat_sq[0:n, m % 2, :].rearrange("p (h d) -> p h d", h=4),
                                  AX_X, ALU.add).then_inc(nat_rs, 1)

            def head_factor(m):
                n = NS if m % TT == 0 else P
                dve.wait_ge(nat_sqrt, m + 1)
                if m >= 2:
                    dve.wait_ge(nat_ready, m - 1)
                dve.reciprocal(n_small[0:n, 4 + m % 2, :], n_small[0:n, 2 + m % 2, :]).then_inc(head_ok, 1)

            split_lo(11, 11)
            dve.wait_ge(glu_done, CT)
            dve.wait_ge(fc_ok, 1)
            sum_taps(2)
            sum_taps(3)
            for m in range(6 * TT):
                if m < 4 * TT:
                    sums(m)
                if 1 <= m < 4 * TT + 1:
                    head_factor(m - 1)
                if m > TT and m % TT in (1, 3):
                    n = N_NAT + 2 * (m // TT - 1) + m % TT // 2 + 4
                    split_lo(n, n)
                conv(CONV_QK if m < 4 * TT else CONV_V)
            split_lo(N_OUT + 2, N_OUT + 2)

            mx, rs, ri = soft[:, 0, :], soft[:, 1, :], soft[:, 2, :]

            def maximum(s):
                dve.wait_ge(s_done, s + 1)
                dve.tensor_reduce(mx[:, s % 4:s % 4 + 1], ps[:, s % 3, 0:P * (s % QT + 1)], AX_X, ALU.max,
                                  negate=True).then_inc(max_done, 1)

            def share(s):
                dve.wait_ge(exp_done, s + 1)
                link(dve.reciprocal(ri[:, s % 4:s % 4 + 1], rs[:, s % 4:s % 4 + 1]))
                n = P * (s % QT + 1)
                dve.tensor_scalar(prob[:, s % 2, 0:n], prob[:, s % 2, 0:n], ri[:, s % 4:s % 4 + 1], None, ALU.mult)\
                   .then_inc(p_ready, 1)

            def pair_lo(p2):
                dve.wait_ge(mh_done, p2 + 1)
                dve.tensor_tensor(A_lo[:, CT + p2, NS:T], ps[:, 5, :], A_hi[:, CT + p2, NS:T].bitcast(F32),
                                  ALU.subtract).then_inc(ml_done, 1)

            def forget_rows():
                dve.wait_ge(fs_done, 1)
                dve.wait_ge(nat_done, 6 * TT)
                dve.tensor_scalar(nf_T[:, :], ps[0:NB * H, 6, 0:KS], -1.0, None, ALU.mult)
                for g in range(2):
                    c0 = NEWC + 4 * NQ * g
                    f_q = ps[0:NB * H, 6, c0:c0 + 4 * NQ].rearrange("p (b a q) -> p b a q", b=4, a=1)
                    cp = dve.tensor_tensor(self_q[:, g, :].rearrange("p (b h q) -> p b h q", b=4, h=H),
                                           f_q.broadcast_to([NB * H, 4, H, NQ]),
                                           sel[:, g, :].rearrange("p (b h q) -> p b h q", b=4, h=H), ALU.mult)
                cp.then_inc(smp_ok, 1)

            def centre(c):
                dve.wait_ge(cm_done, 1)
                dve.scalar_tensor_tensor(out=two(c_f[:, c, :]), in0=ps[:, 6:8, 0:HALF], scalar=-1.0 / DA,
                                         in1=two(c_f[:, c, :]), op0=ALU.mult, op1=ALU.add).then_inc(cx_done, 1)

            for s in range(H * QT):
                maximum(s)
                if s >= 1:
                    share(s - 1)
                if s % (2 * QT) == 3 and s > 2 * QT:
                    pair_lo(s // (2 * QT) - 1)
                if s == 1:
                    forget_rows()
                conv(CONV_ATT)
                if s in (LN_MEAN + 2, LN_MEAN + 3):
                    centre(2 * (s - LN_MEAN - 2))
                    centre(2 * (s - LN_MEAN - 2) + 1)
            assert next_step[0] >= CT * TAPS
            share(H * QT - 1)
            pair_lo(PAIRS - 1)
            dve.wait_ge(cr_done, 1)
            link(dve.reciprocal(r_all[:, :], r_all[:, :]))
            for c in range(CT):
                dve.tensor_tensor(c_f[:, c, :], c_f[:, c, :], r_all[:, :], ALU.mult).then_inc(cy_done, 1)

            def sample_max(g):
                dve.wait_ge(sc_done, 4 * (g + 1))
                dve.tensor_reduce(mx[:, g:g + 1], ps[:, g, 0:KS], AX_X, ALU.max, negate=True).then_inc(smax_done, 1)

            def sample_share(g):
                dve.wait_ge(sexp_done, g + 1)
                link(dve.reciprocal(ri[:, g:g + 1], rs[:, g:g + 1]))
                dve.tensor_scalar(prob_s[:, g, :], prob_s[:, g, :], ri[:, g:g + 1], None, ALU.mult).then_inc(sp_ready, 1)

            for g in range(2):
                sample_max(g)
                sample_share(g)
            for c in range(CT):
                dve.wait_ge(cyh_done, c + 1)
                dve.tensor_tensor(A_lo[:, c, :], c_f[:, c, :], A_hi[:, c, :].bitcast(F32), ALU.subtract).then_inc(cyo_done, 1)

            def own_heads(g):
                dve.wait_ge(spv_done, 4 * (g + 1))
                dve.tensor_tensor(own[:, g, :].rearrange("p (h d) -> p h d", h=H),
                                  ps[:, 5 + g, :].rearrange("p (h d) -> p h d", h=H),
                                  head_is[:, :].rearrange("p (h a) -> p h a", a=1).broadcast_to([P, H, HD]),
                                  ALU.mult).then_inc(own_done, 1)

            def gather_heads(g):
                dve.wait_ge(own_T, g + 1)
                for p2 in range(PAIRS):
                    a_ = dve.tensor_reduce(at_s[:, p2, 16 * g:16 * g + 16].rearrange("p (b q) -> p b q", b=4),
                                           ps[:, 3 + g, P * p2:P * p2 + P].rearrange("p (b h q) -> p b q h", b=4, h=H),
                                           AX_X, ALU.add)
                a_.then_inc(ats_ok, 1)

            def sampled_lo(g):
                dve.wait_ge(mh_done, PAIRS + 1 + g)
                dve.tensor_tensor(A_lo[:, CT:KT, 16 * g:16 * g + 16], at_s[:, :, 16 * g:16 * g + 16],
                                  A_hi[:, CT:KT, 16 * g:16 * g + 16].bitcast(F32), ALU.subtract).then_inc(ml_done, 1)

            own_heads(0)
            gather_heads(0)
            sampled_lo(0)
            own_heads(1)
            gather_heads(1)
            sampled_lo(1)

            def add_to_x(k, n, s):
                dve.wait_ge(tile_done, ordinal(n))
                dve.tensor_tensor(two(xT[:, k, :]), result(s), two(xT[:, k, :]), ALU.add).then_inc(evac_done, 1)

            for j in range(8):
                n = N_OUT + j
                add_to_x(j, n, j % 2)
                split_lo(j + 3, n + 3)
                rest_x(j, V_FFN[0], 1, B_hi, B_lo)

            FFA = [0, 8 * CHUNKS]

            def ffn_chunk(layer, c, last, before_first=None):
                n0, base = N_FF[layer] + 16 * c, FFA[layer] + 8 * c
                if before_first is not None:
                    before_first()
                for j in range(16):
                    n = n0 + j
                    if j < 8:
                        dve.wait_ge(tile_done, ordinal(n))
                        if not (isinstance(base, int) and base + j < 2):
                            dve.wait_ge(ah_done, base + j - 1)
                        dve.scalar_tensor_tensor(out=two(t_f[:, j % 2, :]), in0=result(j % 2), scalar=0.0,
                                                 in1=two(r_all[:, :]), op0=ALU.max, op1=ALU.mult).then_inc(evac_done, 1)
                    else:
                        add_to_x(j - 8, n, j % 2)
                    if not (isinstance(n, int) and n + 3 >= N_END):
                        split_lo(j + 3, n + 3)
                    if j < 8:
                        dve.wait_ge(ah_done, base + j + 1)
                        dve.tensor_tensor(A_lo[:, j, :], a_f[:, j % 2, :], A_hi[:, j, :].bitcast(F32), ALU.subtract)\
                           .then_inc(al_done, 1)
                    elif last and layer == 0:
                        rest_x(j - 8, V_MIX[1], 2, B_hi, B_lo)

            def ffn(layer, index):
                ffn_chunk(layer, 0, False, lambda: invert_r(index))
                with dve.Fori(1, CHUNKS - 1) as c:
                    ffn_chunk(layer, c, False)
                ffn_chunk(layer, CHUNKS - 1, True)

            ffn(0, 1)

            for j in range(16):
                n = N_INC + j
                if j == 0:
                    invert_r(2)
                dve.wait_ge(tile_done, ordinal(n))
                if j >= 2:
                    dve.wait_ge(g_done, j - 1)
                evacuate_to(t_f[:, j % 2, :], j % 2).then_inc(evac_done, 1)
                split_lo(j + 3, n + 3)
                if j == 4:
                    dve.wait_ge(w4_ps, 1)
                    w4 = ps[0:NS, 4, 0:H * NQ].rearrange("p (h a q) -> p h a q", h=H, a=1).broadcast_to([NS, H, NB, NQ])
                    dve.tensor_tensor(ws4[:, :, :, :], w4,
                                      blk4[:, :, :].rearrange("p (a b) q -> p a b q", a=1).broadcast_to([NS, H, NB, NQ]),
                                      ALU.mult).then_inc(w4_ok, 1)
                if j in (8, 9):
                    dve.wait_ge(vm_done, 1)
                    for k in range(4 * (j - 8), 4 * (j - 7)):
                        dve.scalar_tensor_tensor(out=two(v_f[:, k, :]), in0=ps[:, 6:8, 0:HALF], scalar=-1.0 / D,
                                                 in1=two(v_f[:, k, :]), op0=ALU.mult, op1=ALU.add).then_inc(vx_done, 1)
                if j == 10 + SGU_VAR:
                    dve.wait_ge(vr_done, 1)
                    link(dve.reciprocal(ssq[:, :], ssq[:, :]))
                if j >= 10 + SGU_VAR and 3 * (j - 10 - SGU_VAR) < KT:
                    for k in range(3 * (j - 10 - SGU_VAR), min(KT, 3 * (j - 9 - SGU_VAR))):
                        dve.tensor_tensor(v_f[:, k, :], v_f[:, k, :], ssq[:, :], ALU.mult).then_inc(vm2_done, 1)
            for k in range(KT):
                dve.wait_ge(vn_T, 2 * k + 2)
                dve.tensor_copy(vn_s[:, P * k:P * k + P], ps[0:NS, 6 + k % 2, 0:P]).then_inc(vns_ok, 1)

            base = 8 * CHUNKS
            dve.wait_ge(g_done, 16)
            dve.wait_ge(bs_in, 16)
            for h in range(H):
                dve.wait_ge(mix_done, h + 1)
                dve.tensor_tensor(v_f[:, h, NS:T].rearrange("p (c q) -> p c q", c=QT),
                                  ps[:, 4 + h % 2, :].rearrange("p (c q) -> p c q", c=QT),
                                  bs_b[:, h:h + 1, :].broadcast_to([P, QT, P]), ALU.add)
                dve.tensor_tensor(v_f[:, h, 0:NS].rearrange("p (b q) -> p b q", b=NB),
                                  ps[:, 6 + h % 2, 0:NS].rearrange("p (b q) -> p b q", b=NB),
                                  bs_b[:, h:h + 1, 0:NQ].broadcast_to([P, NB, NQ]), ALU.add).then_inc(mix_ok, 1)
                dve.wait_ge(mix_ok, h + 1)
                if h >= 2:
                    dve.wait_ge(gl_done, h - 1)
                dve.tensor_tensor(a_f[:, h % 2, :], u_f[:, h, :], v_f[:, h, :], ALU.mult).then_inc(gm_done, 1)
            for j in range(8):
                n = N_OUTC + j
                add_to_x(j, n, j % 2)
                split_lo(j + 3, n + 3)
                rest_x(j, V_FFN[1], 3, B_hi, B_lo)
            ffn(1, 3)





def kernel(**inputs):
    import numpy as np
    import concourse.bacc as bacc
    from concourse.bass_utils import run_bass_kernel_spmd

    nc = bacc.Bacc("TRN2", target_bir_lowering=False, num_devices=1)
    arrays, ins, outs = {}, {}, {}
    for name in INPUTS:
        a = np.ascontiguousarray(inputs[name])
        arrays[f"in_{name}"] = a
        ins[name] = nc.dram_tensor(f"in_{name}", a.shape, mybir.dt.from_np(a.dtype), kind="ExternalInput").ap()
    shapes = output_shapes({name: inputs[name].shape for name in INPUTS})
    for name, shape in shapes:
        outs[name] = nc.dram_tensor(f"out_{name}", shape, F32, kind="ExternalOutput").ap()
    build(nc, ins, outs)
    r = run_bass_kernel_spmd(nc, [arrays], core_ids=[0])
    return tuple(r.results[0][f"out_{name}"] for name, _ in shapes)
```
